# Optimizing a Trainium2 kernel written in Bass

```python
import jax, jax.numpy as jnp
from jax import lax
import numpy as np

D_MODEL = 1024
BATCH = 1
SEQ = 1024
DEPTH = 1

HEAD_DIM = 64
ROPE_THETA = 10000.0
NORM_EPS = 1e-6
NEG_INF = -1e30
BIG = 1e4
NSA_HEADS = 8
NSA_KV_HEADS = 2
NSA_GROUP = NSA_HEADS // NSA_KV_HEADS
CMP_BLOCK = 32
CMP_STRIDE = 16
CMP_HIDDEN = 256
SLC_BLOCK = 64
SLC_TOPN = 8
SLC_LOCAL = 2
WINDOW = 512
NSA_QCHUNK = 64
DSA_HEADS = 8
IDX_HEADS = 4
IDX_DIM = 64
DSA_TOPK_MAX = 256
DSA_QCHUNK = 128
D_FF = -(-8 * D_MODEL // (3 * 256)) * 256
IN_SPLIT = (
    NSA_HEADS * HEAD_DIM,
    NSA_KV_HEADS * HEAD_DIM,
    NSA_KV_HEADS * HEAD_DIM,
    NSA_KV_HEADS * HEAD_DIM,
    NSA_KV_HEADS * HEAD_DIM,
    NSA_KV_HEADS * HEAD_DIM,
    NSA_KV_HEADS * HEAD_DIM,
    3 * NSA_HEADS,
    DSA_HEADS * HEAD_DIM,
    HEAD_DIM,
    HEAD_DIM,
    IDX_HEADS * IDX_DIM,
    IDX_DIM,
    IDX_HEADS,
    2 * D_MODEL,
)
D_IN = sum(IN_SPLIT)

kernel_name = 'hybrid_nsa_dsa_gated_block'

def rmsnorm(x, g):
    xf = x.astype(jnp.float32)
    y = xf * lax.rsqrt(jnp.mean(xf * xf, axis=-1, keepdims=True) + NORM_EPS)
    return (y * g.astype(jnp.float32)).astype(x.dtype)

def rope(x, positions):
    half = x.shape[-1] // 2
    inv_freq = ROPE_THETA ** (-jnp.arange(half, dtype=jnp.float32) / half)
    ang = positions.astype(jnp.float32)[:, None] * inv_freq[None, :]
    cos = jnp.cos(ang)[None, :, None, :]
    sin = jnp.sin(ang)[None, :, None, :]
    xf = x.astype(jnp.float32)
    x1, x2 = xf[..., :half], xf[..., half:]
    return jnp.concatenate([x1 * cos - x2 * sin, x1 * sin + x2 * cos], axis=-1).astype(x.dtype)

def masked_softmax(s, mask):
    s = jnp.where(mask, s.astype(jnp.float32), NEG_INF)
    p = jax.nn.softmax(s, axis=-1)
    return p * jnp.any(mask, axis=-1, keepdims=True)

def to_chunks(a, size):
    b, s = a.shape[0], a.shape[1]
    return a.reshape(b, s // size, size, *a.shape[2:]).swapaxes(0, 1)

def from_chunks(a):
    a = a.swapaxes(0, 1)
    return a.reshape(a.shape[0], a.shape[1] * a.shape[2], *a.shape[3:])

def compress_tokens(kv, pos_emb, w1, w2):
    b, s, hk, d = kv.shape
    n_rep = CMP_BLOCK // CMP_STRIDE
    n_chunks = s // CMP_STRIDE
    ch = kv.reshape(b, n_chunks, CMP_STRIDE, hk, d)
    blocks = jnp.concatenate([ch[:, r:n_chunks - n_rep + 1 + r] for r in range(n_rep)], axis=2)
    blocks = blocks + pos_emb[None, None, :, None, :]
    flat = blocks.transpose(0, 1, 3, 2, 4).reshape(b, blocks.shape[1], hk, CMP_BLOCK * d)
    return jax.nn.gelu(flat @ w1) @ w2

def nsa_mixer(q, k_cmp, v_cmp, k_slc, v_slc, k_win, v_win, gates, pos_k, w1k, w2k, pos_v, w1v, w2v):
    b, s, h, d = q.shape
    scale = d ** -0.5
    qg = q.reshape(b, s, NSA_KV_HEADS, NSA_GROUP, d)
    t = jnp.arange(s)
    kc = compress_tokens(k_cmp, pos_k, w1k, w2k)
    vc = compress_tokens(v_cmp, pos_v, w1v, w2v)
    n_cmp = kc.shape[1]
    cmp_end = jnp.arange(n_cmp) * CMP_STRIDE + CMP_BLOCK - 1
    cmp_mask = (cmp_end[None, :] <= t[:, None])[None, :, None, None, :]
    p_cmp = masked_softmax(jnp.einsum('bshgd,bnhd->bshgn', qg, kc) * scale, cmp_mask)
    o_cmp = jnp.einsum('bshgn,bnhd->bshgd', p_cmp.astype(vc.dtype), vc)
    n_slc = s // SLC_BLOCK
    ci = jnp.arange(n_cmp)[:, None] * CMP_STRIDE
    sj = jnp.arange(n_slc)[None, :] * SLC_BLOCK
    overlap = ((ci < sj + SLC_BLOCK) & (ci + CMP_BLOCK > sj)).astype(jnp.float32)
    p_slc = jnp.einsum('bshn,nj->bshj', p_cmp.sum(axis=3), overlap)
    cur = (t // SLC_BLOCK)[:, None]
    j = jnp.arange(n_slc)[None, :]
    forced = (j == 0) | ((cur - j >= 0) & (cur - j < SLC_LOCAL))
    admissible = j <= cur
    blk_score = jnp.where(forced[None, :, None, :], BIG, p_slc)
    blk_score = jnp.where(admissible[None, :, None, :], blk_score, NEG_INF)
    n_sel = min(SLC_TOPN, n_slc)
    _, blk_idx = lax.top_k(blk_score, n_sel)
    kb = k_slc.reshape(b, n_slc, SLC_BLOCK, NSA_KV_HEADS, d).transpose(0, 3, 1, 2, 4)
    vb = v_slc.reshape(b, n_slc, SLC_BLOCK, NSA_KV_HEADS, d).transpose(0, 3, 1, 2, 4)
    k_win_pad = jnp.pad(k_win, ((0, 0), (WINDOW, 0), (0, 0), (0, 0)))
    v_win_pad = jnp.pad(v_win, ((0, 0), (WINDOW, 0), (0, 0), (0, 0)))
    bi = jnp.arange(b)[:, None, None, None]
    hi = jnp.arange(NSA_KV_HEADS)[None, None, :, None]
    n_tok = n_sel * SLC_BLOCK

    def chunk(args):
        q_c, idx_c, c = args
        t_c = c * NSA_QCHUNK + jnp.arange(NSA_QCHUNK)
        k_sel = kb[bi, hi, idx_c].reshape(b, NSA_QCHUNK, NSA_KV_HEADS, n_tok, d)
        v_sel = vb[bi, hi, idx_c].reshape(b, NSA_QCHUNK, NSA_KV_HEADS, n_tok, d)
        tok = (idx_c[..., None] * SLC_BLOCK + jnp.arange(SLC_BLOCK)).reshape(b, NSA_QCHUNK, NSA_KV_HEADS, n_tok)
        sel_mask = (tok <= t_c[None, :, None, None])[:, :, :, None, :]
        p = masked_softmax(jnp.einsum('bqhgd,bqhkd->bqhgk', q_c, k_sel) * scale, sel_mask)
        o_slc = jnp.einsum('bqhgk,bqhkd->bqhgd', p.astype(v_sel.dtype), v_sel)
        start = c * NSA_QCHUNK
        kwin = lax.dynamic_slice_in_dim(k_win_pad, start, WINDOW + NSA_QCHUNK, axis=1)
        vwin = lax.dynamic_slice_in_dim(v_win_pad, start, WINDOW + NSA_QCHUNK, axis=1)
        kpos = start - WINDOW + jnp.arange(WINDOW + NSA_QCHUNK)
        dist = t_c[:, None] - kpos[None, :]
        win_mask = ((kpos[None, :] >= 0) & (dist >= 0) & (dist < WINDOW))[None, :, None, None, :]
        p = masked_softmax(jnp.einsum('bqhgd,bkhd->bqhgk', q_c, kwin) * scale, win_mask)
        o_win = jnp.einsum('bqhgk,bkhd->bqhgd', p.astype(vwin.dtype), vwin)
        return o_slc, o_win

    n_chunk = s // NSA_QCHUNK
    o_slc, o_win = lax.map(chunk, (to_chunks(qg, NSA_QCHUNK), to_chunks(blk_idx, NSA_QCHUNK), jnp.arange(n_chunk)))
    g = jax.nn.sigmoid(gates.astype(jnp.float32)).astype(q.dtype).reshape(b, s, 3, NSA_KV_HEADS, NSA_GROUP)[..., None]
    o = g[:, :, 0] * o_cmp + g[:, :, 1] * from_chunks(o_slc) + g[:, :, 2] * from_chunks(o_win)
    return o.reshape(b, s, h * d)

def dsa_mixer(q, k, v, iq, ik, iw):
    b, s, h, d = q.shape
    scale = d ** -0.5
    topk = min(DSA_TOPK_MAX, s // 4)
    key_pos = jnp.arange(s)
    bi = jnp.arange(b)[:, None, None]

    def chunk(args):
        q_c, iq_c, iw_c, c = args
        t_c = c * DSA_QCHUNK + jnp.arange(DSA_QCHUNK)
        idx_logits = jnp.einsum('bqhd,bsd->bqhs', iq_c, ik).astype(jnp.float32) * IDX_DIM ** -0.5
        score = jnp.einsum('bqh,bqhs->bqs', iw_c.astype(jnp.float32), jax.nn.relu(idx_logits))
        score = jnp.where(key_pos[None, None, :] <= t_c[None, :, None], score, NEG_INF)
        _, sel = lax.top_k(score, topk)
        k_sel = k[bi, sel]
        v_sel = v[bi, sel]
        mask = (sel <= t_c[None, :, None])[:, :, None, :]
        p = masked_softmax(jnp.einsum('bqhd,bqkd->bqhk', q_c, k_sel) * scale, mask)
        return jnp.einsum('bqhk,bqkd->bqhd', p.astype(v_sel.dtype), v_sel)

    n_chunk = s // DSA_QCHUNK
    o = lax.map(chunk, (to_chunks(q, DSA_QCHUNK), to_chunks(iq, DSA_QCHUNK), to_chunks(iw, DSA_QCHUNK), jnp.arange(n_chunk)))
    return from_chunks(o).reshape(b, s, h * d)

def setup_inputs(seed: int = 0) -> dict:
    key = jax.random.key(seed)
    ks = jax.random.split(key, 17)
    f32 = jnp.float32

    def w(k, shape, fan_in):
        return jax.random.normal(k, shape, f32) * fan_in ** -0.5

    def gain(k, shape):
        return 1.0 + 0.05 * jax.random.normal(k, shape, f32)

    return {
        'x': jax.random.normal(ks[0], (BATCH, SEQ, D_MODEL), f32),
        'norm_mix': gain(ks[1], (DEPTH, D_MODEL)),
        'w_in': w(ks[2], (DEPTH, D_MODEL, D_IN), D_MODEL),
        'cmp_pos_k': 0.1 * jax.random.normal(ks[3], (DEPTH, CMP_BLOCK, HEAD_DIM), f32),
        'cmp_w1_k': w(ks[4], (DEPTH, CMP_BLOCK * HEAD_DIM, CMP_HIDDEN), CMP_BLOCK * HEAD_DIM),
        'cmp_w2_k': w(ks[5], (DEPTH, CMP_HIDDEN, HEAD_DIM), CMP_HIDDEN),
        'cmp_pos_v': 0.1 * jax.random.normal(ks[6], (DEPTH, CMP_BLOCK, HEAD_DIM), f32),
        'cmp_w1_v': w(ks[7], (DEPTH, CMP_BLOCK * HEAD_DIM, CMP_HIDDEN), CMP_BLOCK * HEAD_DIM),
        'cmp_w2_v': w(ks[8], (DEPTH, CMP_HIDDEN, HEAD_DIM), CMP_HIDDEN),
        'w_branch_nsa': w(ks[9], (DEPTH, NSA_HEADS * HEAD_DIM, D_MODEL), NSA_HEADS * HEAD_DIM),
        'w_branch_dsa': w(ks[10], (DEPTH, DSA_HEADS * HEAD_DIM, D_MODEL), DSA_HEADS * HEAD_DIM),
        'w_out': w(ks[11], (DEPTH, D_MODEL, D_MODEL), D_MODEL),
        'norm_ffn': gain(ks[12], (DEPTH, D_MODEL)),
        'w_gate': w(ks[13], (DEPTH, D_MODEL, D_FF), D_MODEL),
        'w_up': w(ks[14], (DEPTH, D_MODEL, D_FF), D_MODEL),
        'w_down': w(ks[15], (DEPTH, D_FF, D_MODEL), D_FF),
        'norm_final': gain(ks[16], (D_MODEL,)),
    }

def reference(x, norm_mix, w_in, cmp_pos_k, cmp_w1_k, cmp_w2_k, cmp_pos_v, cmp_w1_v, cmp_w2_v, w_branch_nsa, w_branch_dsa, w_out, norm_ffn, w_gate, w_up, w_down, norm_final):
    b, s, _ = x.shape
    positions = jnp.arange(s)
    offsets = np.cumsum(IN_SPLIT)[:-1].tolist()
    h = x
    for layer in range(DEPTH):
        xn = rmsnorm(h, norm_mix[layer])
        z = xn @ w_in[layer]
        (q_a, kc, vc, ksl, vsl, kwn, vwn, g_a, q_b, k_b, v_b, iq, ik, iw, g_merge) = jnp.split(z, offsets, axis=-1)
        kvh = lambda a: a.reshape(b, s, NSA_KV_HEADS, HEAD_DIM)
        q_a = rope(q_a.reshape(b, s, NSA_HEADS, HEAD_DIM), positions)
        kc = rope(kvh(kc), positions)
        ksl = rope(kvh(ksl), positions)
        kwn = rope(kvh(kwn), positions)
        y_a = nsa_mixer(q_a, kc, kvh(vc), ksl, kvh(vsl), kwn, kvh(vwn), g_a,
                        cmp_pos_k[layer], cmp_w1_k[layer], cmp_w2_k[layer],
                        cmp_pos_v[layer], cmp_w1_v[layer], cmp_w2_v[layer])
        q_b = rope(q_b.reshape(b, s, DSA_HEADS, HEAD_DIM), positions)
        k_b = rope(k_b.reshape(b, s, 1, HEAD_DIM), positions)[:, :, 0]
        iq = rope(iq.reshape(b, s, IDX_HEADS, IDX_DIM), positions)
        ik = rope(ik.reshape(b, s, 1, IDX_DIM), positions)[:, :, 0]
        iw = iw * IDX_HEADS ** -0.5
        y_b = dsa_mixer(q_b, k_b, v_b, iq, ik, iw)
        y_a = y_a @ w_branch_nsa[layer]
        y_b = y_b @ w_branch_dsa[layer]
        gate = jax.nn.sigmoid(g_merge.astype(jnp.float32)).astype(h.dtype)
        merged = gate[..., :D_MODEL] * y_a + gate[..., D_MODEL:] * y_b
        h = h + merged @ w_out[layer]
        hn = rmsnorm(h, norm_ffn[layer])
        h = h + (jax.nn.silu(hn @ w_gate[layer]) * (hn @ w_up[layer])) @ w_down[layer]
    return rmsnorm(h, norm_final)


_drawn_inputs = setup_inputs


def setup_inputs(seed=0):
    import zlib

    import numpy as np

    out = dict(_drawn_inputs(seed))
    spreads = {}
    factors = {'norm_mix': 3.323, 'cmp_pos_k': 8.0, 'cmp_pos_v': 3.856, 'norm_ffn': 3.703}
    for name, (base, spread) in spreads.items():
        noise = np.random.default_rng([zlib.crc32(name.encode()), seed]).standard_normal(out[name].shape)
        drawn = base * np.exp(spread * noise) if base else spread * noise
        out[name] = __import__('jax').numpy.asarray(drawn.astype(out[name].dtype))
    for name, factor in factors.items():
        out[name] = (out[name] * factor).astype(out[name].dtype)
    return out
```

```python
from contextlib import ExitStack

import concourse.bass as bass
import numpy as np
from concourse import mybir

F32 = mybir.dt.float32
F32R = mybir.dt.float32r
BF16 = mybir.dt.bfloat16
I32 = mybir.dt.int32
ALU = mybir.AluOpType
ACT = mybir.ActivationFunctionType
X = mybir.AxisListType.X

P = 128
HD = 64
NEG = -1e30
BIG = 1e4
EPS = 1e-6


def nth(keys):
    return {k: n + 1 for n, k in enumerate(keys)}


def hybrid_block(nc, A, out, scratch):
    _, S, D = A["x"].shape
    FF = A["w_gate"].shape[2]
    NT, KT, FT = S // P, D // P, FF // P
    HALF, HT = S // 2, S // 2 // P
    H, KV, G = 8, 2, 4
    IH = 4
    TOPK = 256
    WIN = 512
    SLC, NSLC, TOPN = 64, S // 64, 8
    CSTR, CBLK = 16, 32
    NW = (S - CBLK) // CSTR + 1
    JP = CBLK // 2
    HH = A["cmp_w1_k"].shape[2] // P

    off = np.cumsum([0, 512, 128, 128, 128, 128, 128, 128, 24, 512, 64, 64, 256, 64, 4]).tolist()
    (_, o_kc, _, _, _, o_kwn, _, _, o_qb, o_kb, _, _, _, _, o_gm) = off
    IDX, QB, CMP, WKV, QA = "idx", "qb", "cmp", "win", "qa"
    ORDER = [IDX, QB, CMP, WKV, QA]
    COLS = {IDX: (o_kb, o_gm - o_kb), QB: (o_qb, 512), CMP: (o_kc, 512), WKV: (o_kwn, 280), QA: (0, 512)}
    ROPED = {IDX: [(0, 1), (128, 5)], QB: [(0, 8)], CMP: [(0, 2), (256, 2)], WKV: [(0, 2)], QA: [(0, 8)]}
    QBLK = {IDX: [(128, 4, 2)], QB: [(0, 8, 0)], CMP: [], WKV: [], QA: [(0, 8, 0)]}
    KBLK = {IDX: [(0, 0), (384, 6)], QB: [], CMP: [(256, 0), (320, 2)], WKV: [(0, 0), (64, 2)], QA: []}
    GROUPS = {IDX: [4, 4], QB: [4, 4], CMP: [4, 2], WKV: [4], QA: [4, 4]}

    x_rows = A["x"][0].rearrange("(i p) d -> i p d", p=P)
    out_rows = out[0].rearrange("(i p) d -> i p d", p=P)
    w_in = A["w_in"][0].rearrange("(k p) c -> p k c", p=P)

    ctx = ExitStack()

    def sem(name):
        return ctx.enter_context(nc.semaphore(name))

    def sb(stack, name, shape, dt=F32):
        return stack.enter_context(nc.sbuf_tensor(name, shape, dt))

    base, mix = ExitStack(), ExitStack()
    ident = sb(base, "ident", [P, P])
    stat = sb(base, "stat", [P, 5, 8])
    hstat = sb(base, "h_stat", [P, 4, 5, 4])
    causal = sb(mix, "causal_bias", [P, S], BF16)
    winb = sb(mix, "window_bias", [P, WIN + P], BF16)

    cmpb = sb(mix, "cmp_bias", [P, NT, 64])
    kbT = sb(mix, "kbT", [P, 2, S], F32R)
    v_b = sb(mix, "v_b", [P, NT, HD])
    v_slc = sb(mix, "v_slc", [P, NT, KV * HD])
    v_win = sb(mix, "v_win", [P, NT, KV * HD])
    nsa_gate = sb(mix, "nsa_gate", [P, NT, 3 * H])
    TK = list(range(TOPK // P, NT))
    sc_at = {i: sum(P * (m + 1) for m in TK if m < i) for i in TK}
    score = sb(mix, "score", [P, sum(P * (i + 1) for i in TK)])
    iw = sb(mix, "iw", [P, NT, IH])
    bit_cur = sb(mix, "bit_cur", [P, 8], I32)
    bit_flip = sb(mix, "bit_flip", [P, 8], I32)
    bit_try = sb(mix, "bit_try", [P, 8], I32)
    bit_keep = sb(mix, "bit_keep", [P, 8], I32)
    count = sb(mix, "count", [P, 8])
    need = sb(mix, "need", [P, 8])
    kcvcT = sb(mix, "kcvcT", [P, 2, S])

    def score_of(i):
        return score[:, sc_at[i]:sc_at[i] + P * (i + 1)]

    one = ExitStack()
    xTh = sb(one, "xTh", [P, KT, S], F32R)
    xTl = sb(one, "xTl", [P, KT, S], F32R)
    RAW, RING = 2, 4

    def ring_memory(stack, tag):
        return ([sb(stack, f"{tag}_raw{n}", [P, 1024]) for n in range(RAW)],
                [sb(stack, f"{tag}_hi{n}", [P, 1024], F32R) for n in range(RING)],
                [sb(stack, f"{tag}_lo{n}", [P, 1024], F32R) for n in range(RING)])

    raw1, hi1, lo1 = ring_memory(one, "w1")
    zs = [sb(one, f"z{n}", [P, 512]) for n in range(2)]
    rot = sb(one, "rotated", [P, 512])
    ro = [sb(one, f"roped{n}", [P, 512]) for n in range(2)]
    blk = [sb(one, f"blocks{n}", [P, 8, P], F32R) for n in range(2)]
    kcvc = [sb(one, f"kcvc{n}", [P, 2 * P]) for n in range(2)]
    cosT = sb(one, "cosT", [P, NT, HD])
    sinT = sb(one, "sinT", [P, NT, HD])
    with ExitStack() as s:
        XR = 4
        xr = [sb(s, f"xr{n}", [P, D]) for n in range(XR)]
        xs = [sb(s, f"xs{n}", [P, D]) for n in range(2)]
        gain1 = sb(s, "gain_mix", [P, D])
    with ExitStack() as s:
        iqT = sb(s, "iqT", [P, IH, S], F32R)
        ikT = sb(s, "ikT", [P, 2, S], F32R)
    with ExitStack() as s:
        tq = [sb(s, f"turned{n}", [P, 8, P], F32R) for n in range(2)]
        gst = [sb(s, f"gate_out{n}", [P, 512]) for n in range(2)]
        tk_gt = sb(s, "above", [P, S])
        tk_eq = sb(s, "equal", [P, S])
        tk_cum = sb(s, "equal_so_far", [P, S])
    one.close()

    with ExitStack() as s:
        w1c = [sb(s, f"cmp_w1_{n}", [P, JP, HH * P]) for n in "kv"]
        w2c = [sb(s, f"cmp_w2_{n}", [P, HH, 2, HD]) for n in "kv"]
        posc = [sb(s, f"cmp_pos_{n}", [P, CBLK]) for n in "kv"]
        xc = [sb(s, f"cmp_x_{n}", [P, JP, KV, 64]) for n in "kv"]
        hid_k = sb(s, "cmp_hid_k", [P, HH, KV * 64])
        hid_v = sb(s, "cmp_hid_v", [P, HH, KV, 2, 64])
    att = ExitStack()
    yTh = {"nsa": sb(att, "yTh_nsa", [P, KT // 2, S], F32R)}
    yTl = {"nsa": sb(att, "yTl_nsa", [P, KT // 2, S], F32R)}
    with ExitStack() as s:
        kT = {"slc": sb(s, "kT_slc", [P, KV, 2, S], F32R), "win": sb(s, "kT_win", [P, KV, 2, S], F32R)}
    yTh["dsa"] = sb(att, "yTh_dsa", [P, KT // 2, S], F32R)
    yTl["dsa"] = sb(att, "yTl_dsa", [P, KT // 2, S], F32R)
    work = ExitStack()
    kcm = sb(work, "k_cmp", [P, KV, 2, 64], F32R)
    vbd = sb(work, "v_cmp", [P, KV, P])
    qt = [sb(work, f"q{n}", [P, H, P], F32R) for n in range(2)]
    s_sb = [sb(work, f"s{n}", [P, S]) for n in range(2)]
    PR = 3
    p_sb = [sb(work, f"p{n}", [P, S]) for n in range(PR)]
    pT = [sb(work, f"pT{n}", [P, NT, P]) for n in range(2)]
    slcb = sb(work, "slc_bias", [P, KV, S])
    ya = [sb(work, f"ya{n}", [P, H * HD]) for n in range(2)]
    yt = sb(work, "ytmp", [P, H * HD])
    c_s = sb(work, "c_s", [P, H, 64])
    c_p = sb(work, "c_p", [P, H, 64])
    c_pT = sb(work, "c_pT", [P, 4, P])
    c_st = sb(work, "c_st", [P, 4, H])
    pg = sb(work, "p_group", [P, KV, 68])
    bs = sb(work, "blk_score", [P, KV, NSLC])
    rk = sb(work, "rank", [P, KV, NSLC])
    cmp_a = sb(work, "cmp_above", [P, KV, NSLC, NSLC])
    cmp_b = sb(work, "cmp_equal", [P, KV, NSLC, NSLC])
    free_blk = sb(work, "blk_free", [P, NT, NSLC])
    set_blk = sb(work, "blk_set", [P, NT, NSLC])
    seen = sb(work, "row_sees_window", [P, 1])
    lower = sb(work, "lower_index", [P, NSLC, NSLC])
    nmax = sb(work, "nmax", [P, 3, NT, H])
    psum_p = sb(work, "psum_p", [P, 3, NT, H])
    psum_r = sb(work, "psum_r", [P, 3, NT, H])
    work.close()
    att.close()
    mix.close()

    late = ExitStack()
    raw2, hi2, lo2 = ring_memory(late, "w2")
    hrow = sb(late, "h", [P, NT, D])
    with ExitStack() as s:
        sb(s, "skip_y", [P, 11008])
        mTh = sb(s, "mTh", [P, KT, S], F32R)
        mTl = sb(s, "mTl", [P, KT, S], F32R)
        gl = [sb(s, f"gates{n}", [P, 2, HALF]) for n in range(2)]
        ma = sb(s, "ma", [P, HALF])
        mb = sb(s, "mb", [P, HALF])
        mf = [sb(s, f"merged{n}", [P, HALF]) for n in range(2)]
        xl = [gl[n][:, 0, :] for n in range(2)]
    hTh = sb(late, "hTh", [P, KT, HALF], F32R)
    hTl = sb(late, "hTl", [P, KT, HALF], F32R)
    aTh = sb(late, "aTh", [P, FT, HALF], F32R)
    aTl = sb(late, "aTl", [P, FT, HALF], F32R)
    with ExitStack() as s:
        sg = [sb(s, f"silu{n}", [P, HALF]) for n in range(2)]
        af = [sb(s, f"act{n}", [P, HALF]) for n in range(2)]
    hn = [sb(late, f"hn{n}", [P, D]) for n in range(2)]
    gain2 = sb(late, "gain2", [P, D])
    late.close()
    base.close()

    psA = ctx.enter_context(nc.psum_tensor("psA", [P, 4, 512], F32))
    psT = ctx.enter_context(nc.psum_tensor("psT", [P, 4, 512], F32))
    psA2 = psA[:].rearrange("p (a b) c -> p a (b c)", a=2)

    def chunk_items(src, first, width):
        return [[(src[:, 2 * n:2 * n + 2, first:first + width], 0, 2, width)] for n in range(KT // 2)]

    items1 = sum((chunk_items(w_in, *COLS[c]) for c in ORDER), [])
    NCH = len(items1)
    items1 += [[(w_in[:, :, o_gm + P * j:o_gm + P * (j + 1)], 0, KT, P)] for j in range(2 * KT)]
    wa = A["w_branch_nsa"][0].rearrange("(k p) c -> p k c", p=P)
    wb = A["w_branch_dsa"][0].rearrange("(k p) c -> p k c", p=P)
    wo = A["w_out"][0].rearrange("(k p) c -> p k c", p=P)
    wg = A["w_gate"][0].rearrange("(k p) c -> p k c", p=P)
    wu = A["w_up"][0].rearrange("(k p) c -> p k c", p=P)
    wd = A["w_down"][0].rearrange("(k p) c -> p k c", p=P)
    items2 = [[(w[:, :, P * j:P * (j + 1)], 512 * n, KT // 2, P) for n, w in enumerate((wa, wb))]
              for j in range(KT)]
    items2 += sum((chunk_items(wo, 512 * n, 512) for n in range(2)), [])
    for t in range(2):
        for f in range(FT):
            items2 += [[(w[:, :, P * f:P * (f + 1)], 0, KT, P)] for w in (wg, wu)]
        for n in range(2):
            items2 += [[(wd[:, 2 * a:2 * a + 2, 512 * n:512 * (n + 1)], 0, 2, 512)] for a in range(FT // 2)]
    Z_STEPS, G_STEPS = 8 * len(ORDER), 4 * KT
    free1 = [8 * (n // 4) + 7 if n < NCH else Z_STEPS + 2 * (n - NCH) + 1 for n in range(len(items1))]
    M_STEPS, O_STEPS, F_STEPS = 2 * KT, 2 * NT, FT
    free2 = [2 * j + 1 for j in range(KT)] + [M_STEPS + 8 * (n // 4) + 7 for n in range(8)]
    for t in range(2):
        at = M_STEPS + O_STEPS + 2 * F_STEPS * t
        free2 += [at + n // 2 for n in range(2 * FT)] + [at + FT + n for n in range(FT)]

    class Ring:

        def __init__(self, tag, items, free, raw, hi, lo):
            self.items, self.free, self.raw, self.hi, self.lo = items, free, raw, hi, lo
            self.gone = []
            self.raw_in = [sem(f"{tag}_raw_in{n}") for n in range(RAW)]
            self.hi_done, self.lo_done, self.freed = sem(f"{tag}_hi"), sem(f"{tag}_lo"), sem(f"{tag}_free")
            self.landed, total = [], [0] * RAW
            for n, parts in enumerate(items):
                total[n % RAW] += 16 * len(parts)
                self.landed.append(total[n % RAW])

        def due(self, step, depth):
            return [n for n in range(depth, len(self.items)) if self.free[n - depth] == step]

        def used(self, n):
            parts = self.items[n]
            return parts[-1][1] + parts[-1][2] * parts[-1][3]

        def load(self, sp, n):
            if n >= RAW:
                sp.wait_ge(self.lo_done, n - RAW + 1)
            for src, at, k, w in self.items[n]:
                dst = self.raw[n % RAW][:, at:at + k * w].rearrange("p (k w) -> p k w", k=k)
                sp.dma_start(dst, src).then_inc(self.raw_in[n % RAW], 16)

        def split_hi(self, act, n):
            act.wait_ge(self.raw_in[n % RAW], self.landed[n])
            if n >= RING:
                act.wait_ge(*self.gone[n - RING])
            u = self.used(n)
            nc.scalar.copy(self.hi[n % RING][:, 0:u], self.raw[n % RAW][:, 0:u]).then_inc(self.hi_done, 1)

        def split_lo(self, pool, n):
            pool.wait_ge(self.hi_done, n + 1)
            u = self.used(n)
            nc.gpsimd.tensor_tensor(self.lo[n % RING][:, 0:u], self.raw[n % RAW][:, 0:u],
                                    self.hi[n % RING][:, 0:u].bitcast(F32), ALU.subtract).then_inc(self.lo_done, 1)

        def parts(self, n, k):
            return tuple(x[n % RING][:, 0:self.used(n)].rearrange("p (k w) -> p k w", k=k)
                         for x in (self.hi, self.lo))

    w1 = Ring("w1", items1, free1, raw1, hi1, lo1)
    w2 = Ring("w2", items2, free2, raw2, hi2, lo2)

    zsteps = [(c, i) for c in ORDER for i in range(NT)]
    turned = nth([(q, g) for q, (c, i) in enumerate(zsteps) for g in range(len(GROUPS[c]))])
    spills = nth([q for q, (c, i) in enumerate(zsteps) if c != IDX])
    cmps = nth([q for q, (c, i) in enumerate(zsteps) if c == CMP])
    NA = 2 * NT
    LAST = len(zsteps) - 1
    iunits = [(i, h) for i in TK for h in range(IH)]

    units = []
    for i in range(NT):
        units += [("win", i, h) for h in range(H)] + [("slc", i, h) for h in range(H)]
    NU = len(units)
    units += [("dsa", i, h) for i in range(NT) for h in range(H)]
    BR = {"slc": 0, "win": 1, "dsa": 2}

    def keys_of(a, i):
        n = min(i + 1, WIN // P + 1) if a == "win" else i + 1
        return i + 1 - n, n

    def seg(n):
        return [(c, min(c + 512, n * P)) for c in range(0, n * P, 512)]

    E_LAG, T_LAG, V_LAG, F_LAG, Y_LAG = 1, 2, 3, 4, 5
    STEPS6 = len(units) + Y_LAG + 1

    def at(u):
        return units[u] if 0 <= u < len(units) else (None, None, None)

    groups6, opened, taken = [], [], []
    for u in range(STEPS6):
        if u < NU and u % 16 == 0:
            opened.append(("cs", u // 16))
        if u < NU and u % 16 == 8:
            groups6.append(("cp", u // 16, 0))
        if u < NU and u % 16 == 9:
            opened.append(("co", u // 16))
        a, i, h = at(u - T_LAG)
        if a:
            groups6 += [("p", u - T_LAG, g) for g in range(len(seg(keys_of(a, i)[1])))]
        a, i, h = at(u - V_LAG)
        if a and h == 0:
            opened.append((a, i))
        a, i, h = at(u - Y_LAG)
        if a in ("slc", "dsa") and h == H - 1:
            groups6.append(("y", a, i))
    g6 = {k: n for n, k in enumerate(groups6)}
    o6 = {k: n for n, k in enumerate(opened)}

    def by_act(key):
        return key[0] == "cp" or (key[0] == "p" and (key[1] + key[2]) % 2 == 0)

    act_took = nth([k for k in groups6 if by_act(k)])
    dve_took = nth([k for k in groups6 if not by_act(k)])
    for u in range(STEPS6):
        if u < NU and u % 16 == 0:
            taken.append(("cs", u // 16))
        if u < NU and u % 16 == 10:
            taken.append(("co", u // 16))
        a, i, h = at(u - F_LAG)
        if a and h == H - 1:
            taken.append((a, i))
    o_took = nth(taken)
    ysteps = nth([k for k in groups6 if k[0] == "y"])

    consts = sem("consts")
    x_in = [sem(f"x_in{n}") for n in range(XR)]
    table_in = sem("table_in")
    sq_done, var_done, sd_done, xs_done = sem("sq"), sem("var"), sem("sd"), sem("xs")
    xt_ps, xh_done, xl_done = sem("xt_ps"), sem("xh"), sem("xl")
    z_ps, z_out, rope_done = sem("z_ps"), sem("z_out"), sem("rope")
    bh_done, bl_done = sem("blk_hi"), sem("blk_lo")
    zt_ps, zt_out = sem("zt_ps"), sem("zt_out")
    spilled = [sem(f"spilled{n}") for n in range(2)]
    id_ps, relu_done, sc_done = sem("id_ps"), sem("relu"), sem("score_sum")
    g_ps, g_out = sem("g_ps"), sem("g_out")
    g_stored = [sem(f"g_stored{n}") for n in range(2)]
    bs_done, rank_done = sem("blk_score_done"), sem("rank_done")
    dve_seq, pool_seq = sem("dve_seq"), sem("pool_seq")
    tk_done = sem("topk_bias")
    cw_in, cx_k, cx_v = sem("cw_in"), sem("cx_k"), sem("cx_v")
    ch_ps, ch_out, ck_ps, ck_hi, c_done = sem("ch_ps"), sem("ch_out"), sem("ck_ps"), sem("ck_hi"), sem("c_done")
    kT_in = sem("kT_in")
    q_in = [sem(f"q_in{n}") for n in range(2)]
    s_ps, s_done, p_done = sem("s_ps"), sem("s_done"), sem("p_done")
    t_ps, t_act, t_dve = sem("t_ps"), sem("t_act"), sem("t_dve")
    cs_ps, cs_out, ce_done, cp_done, sb_done = sem("cs_ps"), sem("cs_out"), sem("ce"), sem("cp"), sem("slc_bias_done")
    pv_ps, o_out, y_done, yh_done = sem("pv_ps"), sem("o_out"), sem("y_done"), sem("yh")
    gl_in = [sem(f"gl_in{n}") for n in range(2)]
    m_ps, m_done, mh_done, ml_done = sem("m_ps"), sem("m_done"), sem("mh"), sem("ml")
    xl_in = [sem(f"xl_in{n}") for n in range(2)]
    o_ps, h_done = sem("o_ps"), sem("h_done")
    gain_in = sem("gain_in")
    hq_done, hv_done, hd_done, hn_done = sem("hq"), sem("hv"), sem("hd"), sem("hn_done")
    ht_ps, hh_done, hl_done = sem("ht_ps"), sem("hh"), sem("hl")
    f_ps, sg_done, af_done, ah_done, al_done = sem("f_ps"), sem("sg"), sem("af"), sem("ah"), sem("al")
    d_ps, d_done, out_ready, stored = sem("d_ps"), sem("d_done"), sem("out_ready"), sem("stored")

    qD = {"nsa": scratch["q_nsa"], "dsa": scratch["q_dsa"]}
    kD = {"slc": scratch["k_slc"], "win": scratch["k_win"]}
    gD = scratch["gates"]
    co_ps = sem("co_ps")

    for n in range(len(items1)):
        if n < NCH:
            ch, a = n // 4, n % 4
            w1.gone.append((w1.freed, 3 * ch + a + 1) if a < 3 else (z_ps, 8 * ch + 8))
        else:
            w1.gone.append((g_ps, 2 * (n - NCH) + 2))
    w2.gone = [(m_ps, 2 * j + 2) for j in range(KT)]
    frees = 0
    for n in range(2):
        w2.gone += [(w2.freed, frees + 1), (w2.freed, frees + 2), (w2.freed, frees + 3), (o_ps, NT * (n + 1))]
        frees += 3
    for t in range(2):
        for f in range(FT):
            w2.gone += [(f_ps, FT * t + f + 1)] * 2
        for n in range(2):
            w2.gone += [(w2.freed, frees + a + 1) for a in range(FT // 2 - 1)] + [(d_ps, 8 * t + 4 * n + 4)]
            frees += FT // 2 - 1

    block = ctx.enter_context(nc.Block())

    def tok(i):
        return slice(P * i, P * (i + 1))

    def heads(ap, n):
        return ap.rearrange("p (h d) -> p h d", h=n)

    N_CONST1 = 9
    N_CONST6 = N_CONST1 + 1 + 11

    def windows(eng, n, done):
        for g in range(KV):
            src = kcvcT[HD * g:HD * (g + 1), n, :].rearrange("p (c s) -> p s c", s=CSTR)
            for u in range(2):
                for j in range(2):
                    last = eng.tensor_tensor(
                        xc[n][HD * u:HD * (u + 1), 8 * j:8 * j + 8, g, 0:NW], src[:, u::2, j:j + NW],
                        posc[n][HD * g:HD * (g + 1), CSTR * j + u:CSTR * (j + 1):2].unsqueeze(2).to_broadcast([HD, 8, NW]),
                        ALU.add)
                    last.then_inc(done, 1)

    def evac_p(eng, copy, v, act_side):
        a, i, h = at(v)
        for g, (c0, c1) in enumerate(seg(keys_of(a, i)[1])):
            key = ("p", v, g)
            if by_act(key) != act_side:
                continue
            eng.wait_ge(t_ps, g6[key] + 1)
            if v >= 2:
                eng.wait_ge(pv_ps, v - 1)
            copy(pT[v % 2][:, c0 // P:c1 // P, :].rearrange("p k t -> p (k t)"), psT[:, g6[key] % 2, 0:c1 - c0])\
                .then_inc(t_act if act_side else t_dve, 1)

    @block.sync
    def _(sp):
        def load_x(i):
            if i >= XR:
                sp.wait_ge(xs_done, i - XR + 1)
            sp.dma_start(xr[i % XR][:], x_rows[i]).then_inc(x_in[i % XR], 16)

        for i in range(XR):
            load_x(i)
        sp.dma_start(gain1[:], A["norm_mix"][0:1, :].to_broadcast([P, D])).then_inc(gain_in, 16)
        for n in range(RAW):
            w1.load(sp, n)
        sp.dma_start(cosT[:], A["rope_cos"].rearrange("(i p) d -> p i d", p=P)).then_inc(table_in, 16)
        sp.dma_start(sinT[:], A["rope_sin"].rearrange("(i p) d -> p i d", p=P)).then_inc(table_in, 16)
        for i in range(XR, NT):
            load_x(i)
        for n in range(RAW, RAW + RING):
            w1.load(sp, n)

        def spill(q):
            c, i = zsteps[q]
            if c == IDX:
                return
            sp.wait_ge(zt_out, turned[q, 0] if c in (CMP, WKV) else turned[q, 1])
            n = spills[q] - 1
            t = tq[n % 2]
            if c in (QA, QB):
                dst, src = qD["nsa" if c == QA else "dsa"][i], t[:].rearrange("p b t -> p (b t)")
            else:
                dst, src = kD["slc" if c == CMP else "win"][:, :, tok(i)], t[:, 0:4, :]
            sp.dma_start(dst, src.bitcast(F32)).then_inc(spilled[n % 2], 16)

        for q in range(Z_STEPS + 3):
            if q < Z_STEPS:
                for n in w1.due(q, RAW + RING):
                    w1.load(sp, n)
            if q >= 3:
                spill(q - 3)
        for g in range(G_STEPS):
            for n in w1.due(Z_STEPS + g, RAW + RING):
                w1.load(sp, n)
            sp.wait_ge(g_out, g + 1)
            sp.dma_start(gD[g // 2, :, HALF * (g % 2):HALF * (g % 2 + 1)], gst[g % 2][:])\
                .then_inc(g_stored[g % 2], 16)

        sp.wait_ge(g_ps, G_STEPS)
        sp.wait_ge(w1.lo_done, len(items1))
        sp.wait_ge(bl_done, Z_STEPS)
        sp.wait_ge(zt_ps, len(turned))
        sp.wait_ge(rope_done, Z_STEPS)
        for n, kv in enumerate("kv"):
            sp.dma_start(w1c[n][:], A[f"cmp_w1_{kv}"][0].rearrange("(j p) c -> p j c", p=P)).then_inc(cw_in, 16)
            for r in range(2):
                sp.dma_start(w2c[n][:, :, r, :], A[f"cmp_w2_{kv}"][0].rearrange("(a p) d -> p a d", p=P))\
                    .then_inc(cw_in, 16)
                sp.dma_start(posc[n][HD * r:HD * (r + 1), :], A[f"cmp_pos_{kv}"][0].rearrange("j d -> d j"),
                             allow_slow_non_contiguous=True).then_inc(cw_in, 16)
        for n in range(2):
            sp.wait_ge(spilled[n], 16 * len([s for s in spills.values() if (s - 1) % 2 == n]))
            sp.wait_ge(g_stored[n], 16 * (G_STEPS // 2))
        sp.wait_ge(c_done, 1)
        sp.wait_ge(tk_done, len(TK))
        for a in ("slc", "win"):
            sp.dma_start(kT[a][:].rearrange("p a b s -> p (a b) s").bitcast(F32), kD[a]).then_inc(kT_in, 16)
        for k in range(2 * NT):
            set_, i = ("nsa", k) if k < NT else ("dsa", k - NT)
            if k >= 2:
                sp.wait_ge(s_ps, 16 * (k - 1) if k <= NT + 1 else NU + 8 * (k - 1 - NT))
            sp.dma_start(qt[k % 2][:].rearrange("p h t -> p (h t)").bitcast(F32), qD[set_][i])\
                .then_inc(q_in[k % 2], 16)

        sp.wait_ge(pv_ps, len(units))
        sp.wait_ge(t_dve, len(dve_took))
        for n in range(RAW + RING):
            w2.load(sp, n)
        for m in range(M_STEPS):
            for n in w2.due(m - 2, RAW + RING):
                w2.load(sp, n)
            if m >= 2:
                sp.wait_ge(m_done, m - 1)
            j, half = m // 2, m % 2
            for b in range(2):
                sp.dma_start(gl[m % 2][:, b, :], gD[KT * b + j, :, HALF * half:HALF * (half + 1)])\
                    .then_inc(gl_in[m % 2], 16)
        sp.wait_ge(m_done, M_STEPS)
        for o in range(O_STEPS + 2):
            for n in w2.due(M_STEPS + o - 2, RAW + RING):
                w2.load(sp, n)
            if o >= O_STEPS:
                continue
            if o >= 2:
                sp.wait_ge(h_done, o - 1)
            n, i = o // NT, o % NT
            sp.dma_start(xl[o % 2], x_rows[i][:, 512 * n:512 * (n + 1)]).then_inc(xl_in[o % 2], 16)
        sp.wait_ge(h_done, O_STEPS)
        sp.dma_start(gain2[:], A["norm_ffn"][0:1, :].to_broadcast([P, D])).then_inc(gain_in, 16)
        for t in range(2):
            at_ = M_STEPS + O_STEPS + 2 * FT * t
            for f in range(FT):
                for n in w2.due(at_ + f, RAW + RING):
                    w2.load(sp, n)
            if t == 0:
                sp.wait_ge(hn_done, 2 * HT)
                sp.dma_start(gain2[:], A["norm_final"].rearrange("(a d) -> a d", a=1).to_broadcast([P, D]))\
                    .then_inc(gain_in, 16)
            for a in range(FT):
                for n in w2.due(at_ + FT + a, RAW + RING):
                    w2.load(sp, n)
            for b in range(HT):
                sp.wait_ge(out_ready, HT * t + b + 1)
                sp.dma_start(out_rows[HT * t + b], hrow[:, HT * t + b, :]).then_inc(stored, 16)
        sp.wait_ge(stored, 16 * NT)

    @block.gpsimd
    def _(pool):
        total = [0]

        def made(ins):
            ins.then_inc(consts, 1)
            total[0] += 1
            pool.wait_ge(consts, total[0])

        def select(ap, keep, fill, first, per_row, pattern):
            made(pool.affine_select(out=ap, in_=ap, compare_op=keep, fill=fill, base=first,
                                    pattern=pattern, channel_multiplier=per_row))

        made(pool.memset(ident[:], 0.0))
        select(ident[:], ALU.not_equal, 1.0, 0, 1, [[-1, P]])
        made(pool.memset(causal[:], 0.0))
        select(causal[:, S - P:S], ALU.is_ge, NEG, 0, 1, [[-1, P]])
        made(pool.memset(winb[:], 0.0))
        select(winb[:, WIN:WIN + P], ALU.is_ge, NEG, 0, 1, [[-1, P]])
        select(winb[:, 0:P], ALU.is_gt, NEG, 0, -1, [[1, P]])
        made(pool.memset(cmpb[:], 0.0))
        select(cmpb[:], ALU.is_ge, NEG, 1 - CBLK, 1, [[P, NT], [-CSTR, 64]])
        for n in range(len(items1)):
            w1.split_lo(pool, n)
        pool.wait_ge(cw_in, 16 * 10)
        pool.wait_ge(zt_out, len(turned))
        pool.wait_ge(z_out, Z_STEPS)
        made(pool.memset(xc[1][:, :, :, NW:64], 0.0))
        windows(nc.gpsimd, 1, cx_v)
        pool.wait_ge(c_done, 1)
        made(pool.memset(lower[:], 1.0))
        select(lower[:], ALU.is_gt, 0.0, 0, 0, [[1, NSLC], [-1, NSLC]])
        made(pool.memset(free_blk[:], 1.0))
        select(free_blk[:], ALU.is_ge, 0.0, -2 * SLC, 1, [[P, NT], [-SLC, NSLC]])
        made(pool.memset(free_blk[:, :, 0:1], 0.0))
        made(pool.memset(set_blk[:], BIG))
        select(set_blk[:], ALU.is_ge, NEG, 0, 1, [[P, NT], [-SLC, NSLC]])
        select(set_blk[:, :, 1:NSLC], ALU.is_gt, 0.0, 3 * SLC, -1, [[-P, NT], [SLC, NSLC - 1]])
        made(pool.memset(pg[:], 0.0))
        made(pool.memset(seen[:], 1.0))
        select(seen[:], ALU.is_ge, 0.0, 1 - CBLK, 1, [[0, 1]])
        seq = [0]

        def then(ins):
            ins.then_inc(pool_seq, 1)
            seq[0] += 1
            pool.wait_ge(pool_seq, seq[0])

        def block_bias(i):
            n, w = 2 * (i + 1), P * (i + 1)
            pool.wait_ge(cp_done, i + 1)
            head = c_p[:].rearrange("p (a g) w -> p g a w", a=KV)
            then(nc.gpsimd.tensor_tensor(pg[:, :, 1:65], head[:, 0], head[:, 1], ALU.add))
            for g in range(2, G):
                then(nc.gpsimd.tensor_tensor(pg[:, :, 1:65], pg[:, :, 1:65], head[:, g], ALU.add))
            then(nc.gpsimd.tensor_tensor(bs[:], pg[:, :, 0:64:4], pg[:, :, 1:65:4], ALU.add))
            for k in (2, 3, 4):
                then(nc.gpsimd.tensor_tensor(bs[:], bs[:], pg[:, :, k:k + 64:4], ALU.add))
            then(nc.gpsimd.tensor_tensor(bs[:], bs[:], free_blk[:, i, :].unsqueeze(1).to_broadcast([P, KV, NSLC]), ALU.mult))
            nc.gpsimd.tensor_tensor(bs[:], bs[:], set_blk[:, i, :].unsqueeze(1).to_broadcast([P, KV, NSLC]), ALU.add)\
                .then_inc(bs_done, 1)
            pool.wait_ge(rank_done, i - TOPN // 2 + 1)
            pool.wait_ge(s_done, 16 * i)
            for a in range(KV):
                last = nc.gpsimd.tensor_copy(slcb[:, a, 0:w].rearrange("p (j s) -> p j s", s=SLC),
                                      rk[:, a, 0:n].unsqueeze(2).to_broadcast([P, n, SLC]))
            then(last)
            for a in range(KV):
                last = nc.gpsimd.tensor_tensor(slcb[:, a, w - P:w], slcb[:, a, w - P:w], causal[:, S - P:S], ALU.add)
            last.then_inc(sb_done, 1)

        for i in range(TOPN // 2, NT):
            block_bias(i)
        for n in range(len(items2)):
            w2.split_lo(pool, n)

    @block.scalar
    def _(act):
        a_ = nc.scalar

        for b in range(2):
            for i in range(HT * b, HT * (b + 1)):
                act.wait_ge(x_in[i % XR], 16 * (i // XR + 1))
                if i >= 2:
                    act.wait_ge(sq_done, i - 1)
                a_.activation(blk[i % 2][:].rearrange("p b t -> p (b t)").bitcast(F32), xr[i % XR][:], ACT.Square,
                              accum_out=stat[:, 0, i:i + 1]).then_inc(sq_done, 1)
            act.wait_ge(var_done, b + 1)
            a_.activation(stat[:, 2, HT * b:HT * b + HT], stat[:, 1, HT * b:HT * b + HT], ACT.Sqrt).then_inc(sd_done, 1)
            for n in range(8 * b, 8 * b + 8):
                i, g = n // 2, n % 2
                act.wait_ge(xt_ps, n + 1)
                a_.copy(xTh[:, 4 * g:4 * g + 4, tok(i)], psT[:, n % 4, :].rearrange("p (k t) -> p k t", k=4))\
                    .then_inc(xh_done, 1)
            for n in (2 * b, 2 * b + 1):
                w1.split_hi(act, n)

        def z_evac(q):
            c, i = zsteps[q]
            ps = psA[:, q % 4, :]
            act.wait_ge(z_ps, q + 1)
            if q >= 2:
                act.wait_ge(rope_done, q - 1)
            if c == IDX:
                a_.copy(zs[q % 2][:, 0:448], ps[:, 0:448])
                a_.copy(v_b[:, i, :], ps[:, 64:128])
                last = a_.activation(iw[:, i, :], ps[:, 448:452], ACT.Copy, scale=IH ** -0.5)
            elif c == CMP:
                a_.copy(zs[q % 2][:, 0:384], ps[:, 0:384])
                a_.copy(v_slc[:, i, :], ps[:, 384:512])
                if cmps[q] > 2:
                    act.wait_ge(zt_ps, turned[q - 2, 1])
                last = a_.copy(kcvc[q % 2][:, P:2 * P], ps[:, P:2 * P])
            elif c == WKV:
                a_.copy(zs[q % 2][:, 0:128], ps[:, 0:128])
                a_.copy(v_win[:, i, :], ps[:, 128:256])
                last = a_.activation(nsa_gate[:, i, :], ps[:, 256:280], ACT.Sigmoid)
            else:
                last = a_.copy(zs[q % 2][:], ps)
            last.then_inc(z_out, 1)

        def block_hi(q):
            c, i = zsteps[q]
            act.wait_ge(rope_done, q + 1)
            if q >= 2:
                act.wait_ge(zt_ps, turned[q - 2, len(GROUPS[zsteps[q - 2][0]]) - 1])
            else:
                act.wait_ge(sq_done, NT)
            r, t = ro[q % 2], blk[q % 2]
            for col, n, b in QBLK[c]:
                last = a_.copy(t[:, b:b + n, 0:HD], heads(r[:, col:col + n * HD], n))
            for col, b in KBLK[c]:
                last = a_.copy(t[:, b, :].rearrange("p (r d) -> p r d", r=2),
                               r[:, col:col + HD].unsqueeze(1).to_broadcast([P, 2, HD]))
            last.then_inc(bh_done, 1)

        def turned_out(q):
            c, i = zsteps[q]
            for g, n in enumerate(GROUPS[c]):
                k = turned[q, g]
                ps = psT[:, (NA + k - 1) % 4, :].rearrange("p (b t) -> p b t", b=4)
                if q == 0 and g == 0:
                    act.wait_ge(xt_ps, NA)
                    act.wait_ge(xs_done, NT)
                act.wait_ge(zt_ps, k)
                if c == IDX and g == 0:
                    a_.copy(kbT[:, :, tok(i)], ps[:, 0:2, :])
                    last = a_.copy(iqT[:, 0:2, tok(i)], ps[:, 2:4, :])
                elif c == IDX:
                    a_.copy(iqT[:, 2:4, tok(i)], ps[:, 0:2, :])
                    last = a_.copy(ikT[:, :, tok(i)], ps[:, 2:4, :])
                elif c == CMP and g == 1:
                    last = a_.copy(kcvcT[:, :, tok(i)], ps[:, 0:2, :])
                else:
                    s_ = spills[q] - 1
                    if s_ >= 2 and g == 0:
                        act.wait_ge(spilled[s_ % 2], 16 * (s_ // 2))
                    last = a_.copy(tq[s_ % 2][:, 4 * g:4 * g + 4, :], ps)
                last.then_inc(zt_out, 1)

        def stage2(first, stop):
            for q in range(first, stop + 2):
                if q < stop:
                    for n in w1.due(q, RING):
                        w1.split_hi(act, n)
                    z_evac(q)
                if first <= q - 1 < stop:
                    block_hi(q - 1)
                if first <= q - 2 < stop:
                    turned_out(q - 2)

        stage2(0, NT)
        for v, (i, h) in enumerate(iunits):
            act.wait_ge(id_ps, v + 1)
            ps = psA2[:, v % 2, 0:P * (i + 1)]
            a_.activation(ps, ps, ACT.Relu, scale=HD ** -0.5).then_inc(relu_done, 1)
        act.wait_ge(id_ps, len(iunits))
        stage2(NT, Z_STEPS)
        for g in range(G_STEPS):
            for n in w1.due(Z_STEPS + g, RING):
                w1.split_hi(act, n)
            act.wait_ge(g_ps, g + 1)
            if g >= 2:
                act.wait_ge(g_stored[g % 2], 16 * (g // 2))
            a_.activation(gst[g % 2][:], psA[:, g % 4, :], ACT.Sigmoid).then_inc(g_out, 1)

        act.wait_ge(g_ps, G_STEPS)
        for hh in range(HH):
            act.wait_ge(ch_ps, hh + 1)
            a_.activation(hid_k[:, hh, :], psA[:, hh, 0:P], ACT.Gelu_apprx_tanh).then_inc(ch_out, 1)
        for hh in range(HH):
            act.wait_ge(ch_ps, HH + hh + 1)
            for r in range(2):
                last = a_.activation(hid_v[:, hh, :, r, :], psA[:, HH + hh, 0:P].rearrange("p (g w) -> p g w", g=KV),
                                     ACT.Gelu_apprx_tanh)
            last.then_inc(ch_out, 1)
        act.wait_ge(ck_ps, 1)
        a_.copy(kcm[:, :, 0, :], psT[:, 0, 0:P].rearrange("p (g w) -> p g w", g=KV)).then_inc(ck_hi, 1)

        for u in range(STEPS6):
            v = u - E_LAG
            a, i, h = at(v)
            if a:
                n = P * keys_of(a, i)[1]
                act.wait_ge(s_done, v + 1)
                if v >= PR:
                    b, j, _ = at(v - PR)
                    act.wait_ge(t_ps, g6["p", v - PR, len(seg(keys_of(b, j)[1])) - 1] + 1)
                a_.activation(p_sb[v % PR][:, 0:n], s_sb[v % 2][:, 0:n], ACT.Exp, scale=-1.0,
                              bias=nmax[:, BR[a], i, h:h + 1],
                              accum_out=psum_p[:, BR[a], i, h:h + 1]).then_inc(p_done, 1)
            if u < NU and u % 16 == 0:
                i = u // 16
                act.wait_ge(cs_out, i + 1)
                if i > TOPN // 2:
                    act.wait_ge(sb_done, i - TOPN // 2)
                a_.activation(c_p[:], c_s[:], ACT.Exp, scale=HD ** -0.5).then_inc(ce_done, 1)
            if u < NU and u % 16 == 8:
                i = u // 16
                act.wait_ge(t_ps, g6["cp", i, 0] + 1)
                if i >= 1:
                    act.wait_ge(co_ps, i)
                a_.copy(c_pT[:].rearrange("p a t -> p (a t)"), psT[:, g6["cp", i, 0] % 2, :]).then_inc(t_act, 1)
            v = u - T_LAG
            a, i, h = at(v)
            if a:
                evac_p(act, a_.copy, v, True)
            a, i, h = at(u - Y_LAG)
            if a in ("slc", "dsa") and h == H - 1:
                key = ("y", a, i)
                act.wait_ge(t_ps, g6[key] + 1)
                a_.copy(yTh["dsa" if a == "dsa" else "nsa"][:, :, tok(i)],
                        psT[:, g6[key] % 2, :].rearrange("p (k t) -> p k t", k=4)).then_inc(yh_done, 1)

        for n in range(RING):
            w2.split_hi(act, n)
        for m in range(M_STEPS):
            for n in w2.due(m, RING):
                w2.split_hi(act, n)
            act.wait_ge(m_done, m + 1)
            j, half = m // 2, m % 2
            a_.copy(mTh[:, j, HALF * half:HALF * (half + 1)], mf[m % 2][:]).then_inc(mh_done, 1)
        for o in range(O_STEPS):
            for n in w2.due(M_STEPS + o, RING):
                w2.split_hi(act, n)

        def norm_squares(r, t):
            for b in range(HT):
                if b >= 2:
                    act.wait_ge(hq_done, HT * r + b - 1)
                a_.activation(hn[b % 2][:], hrow[:, HT * t + b, :], ACT.Square, accum_out=hstat[:, r, 0, b:b + 1])\
                    .then_inc(hq_done, 1)
            act.wait_ge(hv_done, r + 1)
            a_.activation(hstat[:, r, 2, :], hstat[:, r, 1, :], ACT.Sqrt).then_inc(hd_done, 1)

        def turn_h(t):
            for n in range(8 * t, 8 * t + 8):
                b, g = n // 2 % HT, n % 2
                act.wait_ge(ht_ps, n + 1)
                if t and n == 8:
                    act.wait_ge(f_ps, FT)
                a_.copy(hTh[:, 4 * g:4 * g + 4, tok(b)], psT[:, n % 4, :].rearrange("p (k t) -> p k t", k=4))\
                    .then_inc(hh_done, 1)

        def act_hi(fc):
            act.wait_ge(af_done, fc + 1)
            if fc >= FT:
                act.wait_ge(d_ps, 8)
            a_.copy(aTh[:, fc % FT, :], af[fc % 2][:]).then_inc(ah_done, 1)

        act.wait_ge(h_done, O_STEPS)
        norm_squares(0, 0)
        turn_h(0)
        for t in range(2):
            step = M_STEPS + O_STEPS + 2 * FT * t
            for f in range(FT):
                fc = FT * t + f
                for n in w2.due(step + f, RING):
                    w2.split_hi(act, n)
                act.wait_ge(f_ps, fc + 1)
                if fc >= 2:
                    act.wait_ge(af_done, fc - 1)
                if f < 2:
                    act.wait_ge(ht_ps, 16 if t else 8)
                    act.wait_ge(hq_done, HT * (3 if t else 1))
                a_.activation(sg[fc % 2][:], psA[:, 2 * (fc % 2), :], ACT.Silu).then_inc(sg_done, 1)
                if f >= 1:
                    act_hi(fc - 1)
            act_hi(FT * t + FT - 1)
            if t == 0:
                act.wait_ge(al_done, FT)
                norm_squares(1, 1)
                turn_h(1)
            for a in range(FT):
                for n in w2.due(step + FT + a, RING):
                    w2.split_hi(act, n)
            act.wait_ge(d_done, 8 * (t + 1))
            if t == 1:
                act.wait_ge(al_done, 2 * FT)
            norm_squares(2 + t, t)

    @block.tensor
    def _(pe):
        def three(ps, pairs, start=True, stop=True):
            for n, ((ah, al), (bh, bl)) in enumerate(pairs):
                first, last = start and n == 0, stop and n == len(pairs) - 1
                pe.matmul(ps, ah, bh, start=first, stop=False)
                pe.matmul(ps, ah, bl, start=False, stop=False)
                mm = pe.matmul(ps, al, bh, start=False, stop=last)
            return mm

        def turn4(bank, blocks):
            for n, src in enumerate(blocks):
                mm = pe.transpose(bank[:, P * n:P * (n + 1)], src, ident[:])
            return mm

        pe.wait_ge(consts, 2)
        for n in range(NA):
            i, g = n // 2, n % 2
            pe.wait_ge(xs_done, i + 1)
            if n >= 4:
                pe.wait_ge(xl_done, n - 3)
            turn4(psT[:, n % 4, :], [xs[i % 2][:, P * k:P * (k + 1)] for k in range(4 * g, 4 * g + 4)]).then_inc(xt_ps, 1)

        def z_step(q):
            c, i = zsteps[q]
            width = COLS[c][1]
            if q >= 4:
                pe.wait_ge(z_out, q - 3)
            if q == NT:
                pe.wait_ge(sc_done, len(iunits))
            if q == 0:
                pe.wait_ge(xl_done, NA)
            for a in range(KT // 2):
                n = 4 * (q // NT) + a
                if i == 0:
                    pe.wait_ge(w1.lo_done, n + 1)
                hi, lo = w1.parts(n, 2)
                mm = three(psA[:, q % 4, 0:width],
                           [((xTh[:, 2 * a + k, tok(i)], xTl[:, 2 * a + k, tok(i)]), (hi[:, k, :], lo[:, k, :]))
                            for k in range(2)], a == 0, a == KT // 2 - 1)
                if i == NT - 1 and a < KT // 2 - 1:
                    mm.then_inc(w1.freed, 1)
            mm.then_inc(z_ps, 1)

        def z_turn(q):
            c, i = zsteps[q]
            pe.wait_ge(bl_done, q + 1)
            for g, n in enumerate(GROUPS[c]):
                k = turned[q, g]
                if k > 4:
                    pe.wait_ge(zt_out, k - 4)
                src = [blk[q % 2][:, 4 * g + b, :].bitcast(F32) for b in range(n)]
                if c == CMP and g == 1:
                    src = [kcvc[q % 2][:, P * b:P * (b + 1)] for b in range(2)]
                turn4(psT[:, (NA + k - 1) % 4, :], src).then_inc(zt_ps, 1)

        def stage2(first, stop):
            for q in range(first, stop + 2):
                if q < stop:
                    z_step(q)
                if first <= q - 2 < stop:
                    z_turn(q - 2)

        def scores(ps, q_, k_hi, k_lo, n):
            for c0, c1 in seg(n):
                pe.matmul(ps[:, c0:c1], q_, k_hi[:, c0:c1], start=True, stop=False)
                mm = pe.matmul(ps[:, c0:c1], q_, k_lo[:, c0:c1], start=False, stop=True)
            return mm

        stage2(0, NT)
        pe.wait_ge(zt_out, turned[NT - 1, 1])
        pe.wait_ge(z_out, NT)
        for v, (i, h) in enumerate(iunits):
            if v >= 2:
                pe.wait_ge(sc_done, v - 1)
            scores(psA2[:, v % 2, :], iqT[:, h, tok(i)], ikT[:, 0, :], ikT[:, 1, :], i + 1).then_inc(id_ps, 1)
        stage2(NT, Z_STEPS)
        for g in range(G_STEPS):
            n, half = NCH + g // 2, slice(HALF * (g % 2), HALF * (g % 2 + 1))
            pe.wait_ge(w1.lo_done, n + 1)
            if g < 4:
                pe.wait_ge(z_out, Z_STEPS - 3 + g)
            else:
                pe.wait_ge(g_out, g - 3)
            hi, lo = w1.parts(n, KT)
            three(psA[:, g % 4, :], [((hi[:, k, :], lo[:, k, :]), (xTh[:, k, half], xTl[:, k, half]))
                                     for k in range(KT)]).then_inc(g_ps, 1)

        pe.wait_ge(g_out, G_STEPS)
        pe.wait_ge(cw_in, 16 * 10)
        for n, done in ((0, cx_k), (1, cx_v)):
            pe.wait_ge(done, 8)
            for hh in range(HH):
                for j in range(JP):
                    mm = pe.matmul(psA[:, HH * n + hh, 0:P], w1c[n][:, j, P * hh:P * (hh + 1)],
                                   xc[n][:, j, :, :].rearrange("p g w -> p (g w)"), start=(j == 0), stop=(j == JP - 1))
                mm.then_inc(ch_ps, 1)
        pe.wait_ge(zt_out, len(turned))
        pe.wait_ge(ch_out, HH)
        for hh in range(HH):
            mm = pe.matmul(psT[:, 0, 0:P], w2c[0][:, hh, :, :].rearrange("p r d -> p (r d)"), hid_k[:, hh, :],
                           start=(hh == 0), stop=(hh == HH - 1))
        mm.then_inc(ck_ps, 1)
        pe.wait_ge(ch_out, 2 * HH)
        for g in range(KV):
            for hh in range(HH):
                mm = pe.matmul(psT[:, 1 + g, 0:HD], hid_v[:, hh, g, :, :].rearrange("p r w -> p (r w)"),
                               w2c[1][:, hh, 0, :], start=(hh == 0), stop=(hh == HH - 1))
            mm.then_inc(ck_ps, 1)

        pe.wait_ge(c_done, 1)

        def group(key):
            n = g6[key]
            if n >= 2:
                before = groups6[n - 2]
                pe.wait_ge(*((t_act, act_took[before]) if by_act(before) else (t_dve, dve_took[before])))
            return psT[:, n % 2, :]

        def accumulator(key):
            n = o6[key]
            if n >= 2:
                pe.wait_ge(o_out, o_took[opened[n - 2]])
            return psT[:, 2 + n % 2, :]

        for u in range(STEPS6):
            if u < NU and u % 16 == 0:
                i = u // 16
                pe.wait_ge(q_in[i % 2], 16 * (i // 2 + 1))
                bank = accumulator(("cs", i))
                for h in range(H):
                    ps, q_ = bank[:, HD * h:HD * (h + 1)], qt[i % 2][:, h, :]
                    pe.matmul(ps, q_, kcm[:, h // G, 0, :], start=True, stop=False)
                    mm = pe.matmul(ps, q_, kcm[:, h // G, 1, :], start=False, stop=True)
                mm.then_inc(cs_ps, 1)
            if u < NU and u % 16 == 8:
                i = u // 16
                pe.wait_ge(cp_done, i + 1)
                turn4(group(("cp", i, 0)), [c_p[:, 2 * n:2 * n + 2, :].rearrange("p a w -> p (a w)") for n in range(4)])\
                    .then_inc(t_ps, 1)
            if u < NU and u % 16 == 9:
                i = u // 16
                pe.wait_ge(t_act, act_took["cp", i, 0])
                bank = accumulator(("co", i))
                for n in range(4):
                    mm = pe.matmul(bank[:, P * n:P * (n + 1)], c_pT[:, n, :], vbd[:, 2 * n // G, :], start=True, stop=True)
                mm.then_inc(co_ps, 1)
            v = u - T_LAG
            a, i, h = at(v)
            if a:
                pe.wait_ge(p_done, v + 1)
                for g, (c0, c1) in enumerate(seg(keys_of(a, i)[1])):
                    turn4(group(("p", v, g)), [p_sb[v % PR][:, c:c + P] for c in range(c0, c1, P)]).then_inc(t_ps, 1)
            a, i, h = at(u)
            if a:
                if u == 0:
                    pe.wait_ge(kT_in, 32)
                if u >= 2:
                    pe.wait_ge(s_done, u - 1)
                k0, n = keys_of(a, i)
                cols = slice(P * k0, P * (k0 + n))
                if a == "dsa":
                    k = NT + i
                    pe.wait_ge(q_in[k % 2], 16 * (k // 2 + 1))
                    mm = scores(psA2[:, u % 2, :], qt[k % 2][:, h, :], kbT[:, 0, cols], kbT[:, 1, cols], n)
                else:
                    kk = kT[a]
                    mm = scores(psA2[:, u % 2, :], qt[i % 2][:, h, :], kk[:, h // G, 0, cols], kk[:, h // G, 1, cols], n)
                mm.then_inc(s_ps, 1)
            v = u - V_LAG
            a, i, h = at(v)
            if a:
                k0, n = keys_of(a, i)
                for g in range(len(seg(n))):
                    key = ("p", v, g)
                    pe.wait_ge(*((t_act, act_took[key]) if by_act(key) else (t_dve, dve_took[key])))
                bank = accumulator((a, i)) if h == 0 else psT[:, 2 + o6[a, i] % 2, :]
                for k in range(n):
                    if a == "dsa":
                        val = v_b[:, k0 + k, :]
                    else:
                        val = (v_slc if a == "slc" else v_win)[:, k0 + k, HD * (h // G):HD * (h // G + 1)]
                    mm = pe.matmul(bank[:, HD * h:HD * (h + 1)], pT[v % 2][:, k, :], val, start=(k == 0), stop=(k == n - 1))
                mm.then_inc(pv_ps, 1)
            a, i, h = at(u - Y_LAG)
            if a in ("slc", "dsa") and h == H - 1:
                key = ("y", a, i)
                pe.wait_ge(*((y_done, i + 1) if a == "slc" else (o_out, o_took[key[1:]])))
                y = ya[(ysteps[key] - 1) % 2]
                turn4(group(key), [y[:, P * k:P * (k + 1)] for k in range(4)]).then_inc(t_ps, 1)

        pe.wait_ge(t_dve, len(dve_took))
        pe.wait_ge(s_done, len(units))
        for m in range(M_STEPS):
            j, half = m // 2, slice(HALF * (m % 2), HALF * (m % 2 + 1))
            pe.wait_ge(w2.lo_done, j + 1)
            if m >= 2:
                pe.wait_ge(m_done, m - 1)
            hi, lo = w2.parts(j, KT)
            for b, set_ in enumerate(("nsa", "dsa")):
                mm = three(psA[:, 2 * (m % 2) + b, :],
                           [((hi[:, 4 * b + k, :], lo[:, 4 * b + k, :]), (yTh[set_][:, k, half], yTl[set_][:, k, half]))
                            for k in range(4)])
            mm.then_inc(m_ps, 1)
        pe.wait_ge(ml_done, M_STEPS)
        pe.wait_ge(m_done, M_STEPS)
        for o in range(O_STEPS):
            n, i = o // NT, o % NT
            if o >= 4:
                pe.wait_ge(h_done, o - 3)
            for a in range(KT // 2):
                item = KT + 4 * n + a
                if i == 0:
                    pe.wait_ge(w2.lo_done, item + 1)
                hi, lo = w2.parts(item, 2)
                mm = three(psA[:, o % 4, :], [((mTh[:, 2 * a + k, tok(i)], mTl[:, 2 * a + k, tok(i)]), (hi[:, k, :], lo[:, k, :]))
                                              for k in range(2)], a == 0, a == KT // 2 - 1)
                if i == NT - 1 and a < KT // 2 - 1:
                    mm.then_inc(w2.freed, 1)
            mm.then_inc(o_ps, 1)

        def turn_h(t):
            for n in range(8 * t, 8 * t + 8):
                b, g = n // 2, n % 2
                pe.wait_ge(hn_done, b + 1)
                if n >= 4:
                    pe.wait_ge(hl_done, n - 3)
                turn4(psT[:, n % 4, :], [hn[b % 2][:, P * k:P * (k + 1)] for k in range(4 * g, 4 * g + 4)])\
                    .then_inc(ht_ps, 1)

        turn_h(0)
        pe.wait_ge(h_done, O_STEPS)
        item = KT + 8
        for t in range(2):
            pe.wait_ge(hl_done, 8 * (t + 1))
            if t:
                pe.wait_ge(d_done, 4)
            for f in range(FT):
                fc = FT * t + f
                if fc >= 2:
                    pe.wait_ge(af_done, fc - 1)
                for b in range(2):
                    pe.wait_ge(w2.lo_done, item + 1)
                    hi, lo = w2.parts(item, KT)
                    mm = three(psA[:, 2 * (fc % 2) + b, :],
                               [((hi[:, k, :], lo[:, k, :]), (hTh[:, k, :], hTl[:, k, :])) for k in range(KT)])
                    item += 1
                mm.then_inc(f_ps, 1)
            if t == 0:
                turn_h(1)
            pe.wait_ge(al_done, FT * (t + 1))
            for n in range(2):
                if n == 0:
                    pe.wait_ge(af_done, FT * (t + 1))
                else:
                    pe.wait_ge(hl_done, 16)
                    if t:
                        pe.wait_ge(d_done, 8)
                banks = psA if n == 0 else psT
                for a in range(FT // 2):
                    pe.wait_ge(w2.lo_done, item + 1)
                    hi, lo = w2.parts(item, 2)
                    end = a == FT // 2 - 1
                    for b in range(HT):
                        mm = three(banks[:, b, :],
                                   [((aTh[:, 2 * a + k, tok(b)], aTl[:, 2 * a + k, tok(b)]), (hi[:, k, :], lo[:, k, :]))
                                    for k in range(2)], a == 0, end)
                        if end:
                            mm.then_inc(d_ps, 1)
                    if not end:
                        mm.then_inc(w2.freed, 1)
                    item += 1

    @block.vector
    def _(dve):
        v_ = nc.vector
        seq = [0]

        def signal(ins):
            ins.then_inc(dve_seq, 1)
            seq[0] += 1
            return seq[0]

        def then(ins):
            ins.then_inc(dve_seq, 1)
            seq[0] += 1
            dve.wait_ge(dve_seq, seq[0])

        def rstd(st, c):
            then(v_.reciprocal(st[:, 3, c], st[:, 2, c]))
            then(v_.tensor_tensor(st[:, 4, c], st[:, 3, c], st[:, 3, c], ALU.mult))
            then(v_.tensor_tensor(st[:, 4, c], st[:, 4, c], st[:, 1, c], ALU.mult))
            then(v_.tensor_scalar(st[:, 4, c], st[:, 4, c], -0.5, 1.5, ALU.mult, ALU.add))
            then(v_.tensor_tensor(st[:, 3, c], st[:, 3, c], st[:, 4, c], ALU.mult))

        def x_lo(i):
            for n in (2 * i, 2 * i + 1):
                g = n % 2
                dve.wait_ge(xh_done, n + 1)
                v_.tensor_tensor(xTl[:, 4 * g:4 * g + 4, tok(i)], psT[:, n % 4, :].rearrange("p (k t) -> p k t", k=4),
                                 xTh[:, 4 * g:4 * g + 4, tok(i)].bitcast(F32), ALU.subtract).then_inc(xl_done, 1)

        for b in range(2):
            c = slice(HT * b, HT * (b + 1))
            dve.wait_ge(sq_done, HT * (b + 1))
            v_.tensor_scalar(stat[:, 1, c], stat[:, 0, c], 1.0 / D, EPS, ALU.mult, ALU.add).then_inc(var_done, 1)
            dve.wait_ge(var_done, b + 1)
            dve.wait_ge(sd_done, b + 1)
            rstd(stat, c)
            for i in range(HT * b, HT * (b + 1)):
                if i == 0:
                    dve.wait_ge(gain_in, 16)
                if i >= 2:
                    dve.wait_ge(xt_ps, 2 * (i - 1))
                v_.scalar_tensor_tensor(out=xs[i % 2][:], in0=xr[i % XR][:], scalar=stat[:, 3, i:i + 1], in1=gain1[:],
                                        op0=ALU.mult, op1=ALU.mult).then_inc(xs_done, 1)
                if i % HT:
                    x_lo(i - 1)
            x_lo(HT * b + HT - 1)

        def rope(q):
            c, i = zsteps[q]
            z, r = zs[q % 2], ro[q % 2]
            dve.wait_ge(z_out, q + 1)
            if q == 0:
                dve.wait_ge(table_in, 32)
            if q >= 1:
                dve.wait_ge(rope_done, q)
            if q >= 2:
                dve.wait_ge(bh_done, q - 1)
                dve.wait_ge(bl_done, q - 1)
            if c == CMP and cmps[q] > 2:
                dve.wait_ge(zt_ps, turned[q - 2, 1])

            def out_of(col, w):
                return (kcvc[q % 2] if c == CMP and col == 0 else r)[:, col:col + w]

            for col, n in ROPED[c]:
                w = n * HD
                src, tmp = heads(z[:, col:col + w], n), heads(rot[:, col:col + w], n)
                cos = cosT[:, i, :].unsqueeze(1).to_broadcast([P, n, HD])
                v_.tensor_tensor(heads(out_of(col, w), n), src, cos, ALU.mult)
                for lo_, hi_ in ((0, HD // 2), (HD // 2, 0)):
                    sin = sinT[:, i, lo_:lo_ + HD // 2].unsqueeze(1).to_broadcast([P, n, HD // 2])
                    last = v_.tensor_tensor(tmp[:, :, lo_:lo_ + HD // 2], src[:, :, hi_:hi_ + HD // 2], sin, ALU.mult)
            then(last)
            for col, n in ROPED[c]:
                w = n * HD
                last = v_.tensor_tensor(out_of(col, w), out_of(col, w), rot[:, col:col + w], ALU.add)
            last.then_inc(rope_done, 1)

        def block_lo(q):
            c, i = zsteps[q]
            r, t = ro[q % 2], blk[q % 2]
            dve.wait_ge(rope_done, q + 1)
            dve.wait_ge(bh_done, q + 1)
            for col, n, b in QBLK[c]:
                last = v_.tensor_tensor(t[:, b:b + n, HD:P], heads(r[:, col:col + n * HD], n),
                                        t[:, b:b + n, 0:HD].bitcast(F32), ALU.subtract)
            for col, b in KBLK[c]:
                last = v_.tensor_tensor(t[:, b + 1, :].rearrange("p (r d) -> p r d", r=2),
                                        r[:, col:col + HD].unsqueeze(1).to_broadcast([P, 2, HD]),
                                        t[:, b, :].bitcast(F32).rearrange("p (r d) -> p r d", r=2), ALU.subtract)
            last.then_inc(bl_done, 1)

        for q in range(NT + 1):
            if q < NT:
                rope(q)
            if q >= 1:
                block_lo(q - 1)
        dve.wait_ge(consts, N_CONST1)
        for v, (i, h) in enumerate(iunits):
            dve.wait_ge(relu_done, v + 1)
            if v >= 1:
                dve.wait_ge(sc_done, v)
            n = P * (i + 1)
            v_.scalar_tensor_tensor(out=score_of(i), in0=psA2[:, v % 2, 0:n], scalar=iw[:, i, h:h + 1],
                                    in1=causal[:, S - n:S] if h == 0 else score_of(i),
                                    op0=ALU.mult, op1=ALU.add).then_inc(sc_done, 1)

        NTK = len(TK)
        R = slice(0, NTK)

        def counts(threshold):
            done = []
            for n, i in enumerate(TK):
                if n >= 2:
                    dve.wait_ge(dve_seq, done[n - 2])
                done.append(signal(v_.tensor_scalar((tk_gt, tk_eq)[n % 2][:, 0:P * (i + 1)], score_of(i), threshold(n),
                                                    None, ALU.is_ge, ALU.add, accum_out=count[:, n:n + 1])))
            dve.wait_ge(dve_seq, done[-1])

        def bisect_start():
            dve.wait_ge(sc_done, len(iunits))
            counts(lambda n: 0.0)
            v_.memset(bit_cur[:], 0)
            then(v_.tensor_scalar(bit_flip[:, R], count[:, R], float(TOPK), -1.0, ALU.is_lt, ALU.mult))

        def bisect(bit):
            then(v_.tensor_scalar(bit_try[:, R], bit_cur[:, R], 1 << bit, None, ALU.bitwise_or))
            then(v_.tensor_tensor(bit_try[:, R], bit_try[:, R], bit_flip[:, R], ALU.bitwise_xor))
            counts(lambda n: bit_try[:, n:n + 1].bitcast(F32))
            then(v_.tensor_scalar(bit_keep[:, R], count[:, R], float(TOPK), float(1 << bit), ALU.is_ge, ALU.mult))
            then(v_.tensor_tensor(bit_cur[:, R], bit_cur[:, R], bit_keep[:, R], ALU.bitwise_or))

        def selection():
            then(v_.tensor_tensor(bit_try[:, R], bit_cur[:, R], bit_flip[:, R], ALU.bitwise_xor))
            for n, i in enumerate(TK):
                w, t = P * (i + 1), bit_try[:, n:n + 1].bitcast(F32)
                v_.tensor_scalar(tk_gt[:, 0:w], score_of(i), t, None, ALU.is_gt, ALU.add, accum_out=count[:, n:n + 1])
                then(v_.tensor_scalar(tk_eq[:, 0:w], score_of(i), t, None, ALU.is_equal))
                v_.tensor_scalar(need[:, n:n + 1], count[:, n:n + 1], -1.0, float(TOPK), ALU.mult, ALU.add)
                then(v_.tensor_tensor_scan(tk_cum[:, 0:w], tk_eq[:, 0:w], tk_eq[:, 0:w], 0.0, ALU.add, ALU.max))
                then(v_.scalar_tensor_tensor(out=tk_eq[:, 0:w], in0=tk_cum[:, 0:w], scalar=need[:, n:n + 1],
                                             in1=tk_eq[:, 0:w], op0=ALU.is_le, op1=ALU.mult))
                then(v_.tensor_tensor(tk_gt[:, 0:w], tk_gt[:, 0:w], tk_eq[:, 0:w], ALU.add))
                last = v_.tensor_scalar(score_of(i), tk_gt[:, 0:w], 1.0, -NEG, ALU.subtract, ALU.mult)
                last.then_inc(tk_done, 1)
                dve.wait_ge(tk_done, n + 1)

        bisect_start()
        bit = 30
        for q in range(NT, Z_STEPS + 1):
            if q < Z_STEPS:
                rope(q)
            if q > NT:
                block_lo(q - 1)
            if q % 2 == 0 and bit >= 0:
                bisect(bit)
                bit -= 1
        while bit >= 0:
            bisect(bit)
            bit -= 1
        selection()

        dve.wait_ge(cw_in, 16 * 10)
        dve.wait_ge(zt_out, len(turned))
        then(v_.memset(xc[0][:, :, :, NW:64], 0.0))
        windows(v_, 0, cx_k)
        then(v_.memset(vbd[:], 0.0))
        dve.wait_ge(ck_hi, 1)
        v_.tensor_tensor(kcm[:, :, 1, :], psT[:, 0, 0:P].rearrange("p (g w) -> p g w", g=KV),
                         kcm[:, :, 0, :].bitcast(F32), ALU.subtract)
        dve.wait_ge(ck_ps, 1 + KV)
        for g in range(KV):
            for r in range(2):
                rows = slice(HD * r, HD * (r + 1))
                last = v_.tensor_copy(vbd[rows, g, HD * r:HD * (r + 1)], psT[rows, 1 + g, 0:HD])
        last.then_inc(c_done, 1)

        def cmp_scores(i):
            n = o6["cs", i]
            dve.wait_ge(cs_ps, i + 1)
            if i == 0:
                dve.wait_ge(consts, N_CONST6)
            v_.tensor_tensor(c_s[:], heads(psT[:, 2 + n % 2, :], H),
                             cmpb[:, i, :].unsqueeze(1).to_broadcast([P, H, 64]), ALU.add).then_inc(o_out, 1)
            dve.wait_ge(o_out, o_took["cs", i])
            then(v_.tensor_reduce(c_st[:, 0, :], c_s[:], X, ALU.max))
            v_.tensor_tensor(c_s[:], c_s[:], c_st[:, 0, :].unsqueeze(2).to_broadcast([P, H, 64]), ALU.subtract)\
                .then_inc(cs_out, 1)

        def cmp_probs(i):
            dve.wait_ge(ce_done, i + 1)
            then(v_.tensor_reduce(c_st[:, 1, :], c_p[:], X, ALU.add))
            then(v_.reciprocal(c_st[:, 2, :], c_st[:, 1, :]))
            if i == 0:
                then(v_.tensor_scalar(c_st[:, 2, :], c_st[:, 2, :], seen[:, 0:1], None, ALU.mult))
            v_.tensor_tensor(c_p[:], c_p[:], c_st[:, 2, :].unsqueeze(2).to_broadcast([P, H, 64]), ALU.mult)\
                .then_inc(cp_done, 1)

        def block_ranks(i):
            dve.wait_ge(bs_done, i - TOPN // 2 + 1)
            for a in range(KV):
                other = bs[:, a, :].unsqueeze(1).to_broadcast([P, NSLC, NSLC])
                own = bs[:, a, :].unsqueeze(2).to_broadcast([P, NSLC, NSLC])
                v_.tensor_tensor(cmp_a[:, a], other, own, ALU.is_gt)
                last = v_.tensor_tensor(cmp_b[:, a], other, own, ALU.is_equal)
            then(last)
            for a in range(KV):
                last = v_.tensor_tensor(cmp_b[:, a], cmp_b[:, a], lower[:], ALU.mult)
            then(last)
            then(v_.tensor_tensor(cmp_a[:], cmp_a[:], cmp_b[:], ALU.add))
            then(v_.tensor_reduce(rk[:], cmp_a[:], X, ALU.add))
            v_.tensor_scalar(rk[:], rk[:], TOPN - 0.5, NEG, ALU.is_gt, ALU.mult).then_inc(rank_done, 1)

        def unit_scores(u):
            a, i, h = at(u)
            w = P * keys_of(a, i)[1]
            if a == "win":
                bias = winb[:, WIN + P - w:WIN + P]
            elif a == "slc" and 2 * (i + 1) > TOPN:
                bias = slcb[:, h // G, 0:w]
                dve.wait_ge(sb_done, i - TOPN // 2 + 1)
            elif a == "dsa" and i in sc_at:
                bias = score_of(i)
            else:
                bias = causal[:, S - w:S]
            dve.wait_ge(s_ps, u + 1)
            if u >= 2:
                dve.wait_ge(p_done, u - 1)
            v_.tensor_tensor_reduce(out=s_sb[u % 2][:, 0:w], in0=psA2[:, u % 2, 0:w], in1=bias, scale=-(HD ** -0.5),
                                    scalar=3e38, op0=ALU.add, op1=ALU.min,
                                    accum_out=nmax[:, BR[a], i, h:h + 1]).then_inc(s_done, 1)

        def finish(a, i):
            ps = heads(psT[:, 2 + o6[a, i] % 2, :], H)
            key = ("y", "slc" if a == "win" else a, i)
            y = ya[(ysteps[key] - 1) % 2]
            r = psum_r[:, BR[a], i, :]
            dve.wait_ge(pv_ps, units.index((a, i, H - 1)) + 1)
            then(v_.reciprocal(r, psum_p[:, BR[a], i, :]))
            if a == "dsa":
                if ysteps[key] > 2:
                    dve.wait_ge(t_ps, g6[groups_y[ysteps[key] - 3]] + 1)
                v_.tensor_tensor(heads(y[:], H), ps, r.unsqueeze(2).to_broadcast([P, H, HD]), ALU.mult).then_inc(o_out, 1)
                return
            branch = 1 if a == "slc" else 2
            then(v_.tensor_tensor(r, r, nsa_gate[:, i, H * branch:H * (branch + 1)], ALU.mult))
            v_.tensor_tensor(heads(yt[:], H), ps, r.unsqueeze(2).to_broadcast([P, H, HD]), ALU.mult).then_inc(o_out, 1)
            dve.wait_ge(o_out, o_took[a, i])
            add = v_.tensor_tensor(y[:], y[:], yt[:], ALU.add)
            if a == "slc":
                add.then_inc(y_done, 1)
            else:
                then(add)

        groups_y = list(ysteps)
        for u in range(STEPS6):
            if at(u - T_LAG)[0]:
                evac_p(dve, v_.tensor_copy, u - T_LAG, False)
            if u < NU and u % 16 == 0:
                cmp_scores(u // 16)
            if at(u)[0]:
                unit_scores(u)
            if u < NU and u % 16 == 1:
                cmp_probs(u // 16)
            if u < NU and u % 16 == 4 and u // 16 >= TOPN // 2:
                block_ranks(u // 16)
            if u < NU and u % 16 == 10:
                i = u // 16
                key = ("y", "slc", i)
                dve.wait_ge(co_ps, i + 1)
                if ysteps[key] > 2:
                    dve.wait_ge(t_ps, g6[groups_y[ysteps[key] - 3]] + 1)
                v_.tensor_tensor(heads(ya[(ysteps[key] - 1) % 2][:], H), heads(psT[:, 2 + o6["co", i] % 2, :], H),
                                 nsa_gate[:, i, 0:H].unsqueeze(2).to_broadcast([P, H, HD]), ALU.mult).then_inc(o_out, 1)
                dve.wait_ge(o_out, o_took["co", i])
            a, i, h = at(u - F_LAG)
            if a and h == H - 1:
                finish(a, i)
            a, i, h = at(u - Y_LAG)
            if a in ("slc", "dsa") and h == H - 1:
                key = ("y", a, i)
                set_ = "dsa" if a == "dsa" else "nsa"
                dve.wait_ge(yh_done, ysteps[key])
                v_.tensor_tensor(yTl[set_][:, :, tok(i)], psT[:, g6[key] % 2, :].rearrange("p (k t) -> p k t", k=4),
                                 yTh[set_][:, :, tok(i)].bitcast(F32), ALU.subtract).then_inc(t_dve, 1)

        def merged_lo(m):
            j, half = m // 2, slice(HALF * (m % 2), HALF * (m % 2 + 1))
            dve.wait_ge(mh_done, m + 1)
            v_.tensor_tensor(mTl[:, j, half], mf[m % 2][:], mTh[:, j, half].bitcast(F32), ALU.subtract).then_inc(ml_done, 1)

        for m in range(M_STEPS):
            dve.wait_ge(m_ps, m + 1)
            dve.wait_ge(gl_in[m % 2], 32 * (m // 2 + 1))
            if m >= 1:
                dve.wait_ge(m_done, m)
            v_.tensor_tensor(ma[:], psA[:, 2 * (m % 2), :], gl[m % 2][:, 0, :], ALU.mult)
            then(v_.tensor_tensor(mb[:], psA[:, 2 * (m % 2) + 1, :], gl[m % 2][:, 1, :], ALU.mult))
            if m >= 2:
                dve.wait_ge(mh_done, m - 1)
                dve.wait_ge(ml_done, m - 1)
            v_.tensor_tensor(mf[m % 2][:], ma[:], mb[:], ALU.add).then_inc(m_done, 1)
            if m >= 1:
                merged_lo(m - 1)
        merged_lo(M_STEPS - 1)
        for o in range(O_STEPS):
            n, i = o // NT, o % NT
            dve.wait_ge(o_ps, o + 1)
            dve.wait_ge(xl_in[o % 2], 16 * (o // 2 + 1))
            v_.tensor_tensor(hrow[:, i, 512 * n:512 * (n + 1)], psA[:, o % 4, :], xl[o % 2], ALU.add).then_inc(h_done, 1)

        def norm(r, t):
            dve.wait_ge(hq_done, HT * (r + 1))
            v_.tensor_scalar(hstat[:, r, 1, :], hstat[:, r, 0, :], 1.0 / D, EPS, ALU.mult, ALU.add).then_inc(hv_done, 1)
            dve.wait_ge(hv_done, r + 1)
            dve.wait_ge(hd_done, r + 1)
            rstd(hstat[:, r], slice(0, HT))
            dve.wait_ge(gain_in, 16 * min(r + 2, 3) if r != 1 else 32)
            for b in range(HT):
                i = HT * t + b
                if r < 2:
                    if b >= 2:
                        dve.wait_ge(ht_ps, 8 * t + 2 * (b - 1))
                    v_.scalar_tensor_tensor(out=hn[b % 2][:], in0=hrow[:, i, :], scalar=hstat[:, r, 3, b:b + 1], in1=gain2[:],
                                            op0=ALU.mult, op1=ALU.mult).then_inc(hn_done, 1)
                    if b >= 1:
                        h_lo(t, b - 1)
                else:
                    v_.scalar_tensor_tensor(out=hrow[:, i, :], in0=hrow[:, i, :], scalar=hstat[:, r, 3, b:b + 1],
                                            in1=gain2[:], op0=ALU.mult, op1=ALU.mult).then_inc(out_ready, 1)
            if r < 2:
                h_lo(t, HT - 1)

        def h_lo(t, b):
            for g in range(2):
                n = 8 * t + 2 * b + g
                dve.wait_ge(hh_done, n + 1)
                v_.tensor_tensor(hTl[:, 4 * g:4 * g + 4, tok(b)], psT[:, n % 4, :].rearrange("p (k t) -> p k t", k=4),
                                 hTh[:, 4 * g:4 * g + 4, tok(b)].bitcast(F32), ALU.subtract).then_inc(hl_done, 1)

        def act_lo(fc):
            dve.wait_ge(ah_done, fc + 1)
            v_.tensor_tensor(aTl[:, fc % FT, :], af[fc % 2][:], aTh[:, fc % FT, :].bitcast(F32), ALU.subtract)\
                .then_inc(al_done, 1)

        norm(0, 0)
        for t in range(2):
            for f in range(FT):
                fc = FT * t + f
                dve.wait_ge(sg_done, fc + 1)
                if fc >= 2:
                    dve.wait_ge(ah_done, fc - 1)
                    dve.wait_ge(al_done, fc - 1)
                v_.tensor_tensor(af[fc % 2][:], sg[fc % 2][:], psA[:, 2 * (fc % 2) + 1, :], ALU.mult).then_inc(af_done, 1)
                if f >= 1:
                    act_lo(fc - 1)
            act_lo(FT * t + FT - 1)
            if t == 0:
                norm(1, 1)
            for n in range(2):
                for b in range(HT):
                    dve.wait_ge(d_ps, 8 * t + 4 * n + b + 1)
                    piece = hrow[:, HT * t + b, 512 * n:512 * (n + 1)]
                    v_.tensor_tensor(piece, piece, (psA if n == 0 else psT)[:, b, :], ALU.add).then_inc(d_done, 1)
            dve.wait_ge(d_done, 8 * (t + 1))
            norm(2 + t, t)

    ctx.close()


INS = ["x", "norm_mix", "w_in", "cmp_pos_k", "cmp_w1_k", "cmp_w2_k", "cmp_pos_v", "cmp_w1_v", "cmp_w2_v",
       "w_branch_nsa", "w_branch_dsa", "w_out", "norm_ffn", "w_gate", "w_up", "w_down", "norm_final"]


def rope_tables(seq):
    half = HD // 2
    freq = (10000.0 ** (-np.arange(half, dtype=np.float64) / half)).astype(np.float32)
    angle = np.arange(seq, dtype=np.float32)[:, None] * freq[None, :]
    cos, sin = np.cos(angle), np.sin(angle)
    return np.concatenate([cos, cos], 1), np.concatenate([-sin, sin], 1)


def kernel(**inputs):
    import concourse.bacc as bacc
    from concourse.bass_utils import run_bass_kernel_spmd

    nc = bacc.Bacc("TRN2", target_bir_lowering=False, num_devices=1)
    arrays = {name: np.ascontiguousarray(inputs[name]) for name in INS}
    seq, d = arrays["x"].shape[1:]
    arrays["rope_cos"], arrays["rope_sin"] = rope_tables(seq)
    feeds = {f"in_{name}_dram": a for name, a in arrays.items()}
    A = {name: nc.dram_tensor(f"in_{name}_dram", a.shape, F32, kind="ExternalInput").ap() for name, a in arrays.items()}
    out = nc.dram_tensor("out_dram", (1, seq, d), F32, kind="ExternalOutput").ap()
    nt = seq // P
    scratch = {name: nc.dram_tensor(f"scratch_{name}", shape, F32, kind="Internal").ap() for name, shape in {
        "q_nsa": (nt, P, 8 * P), "q_dsa": (nt, P, 8 * P), "k_slc": (P, 4, seq), "k_win": (P, 4, seq),
        "gates": (2 * d // P, P, seq)}.items()}
    hybrid_block(nc, A, out, scratch)
    r = run_bass_kernel_spmd(nc, [feeds], core_ids=[0])
    return np.asarray(r.results[0]["out_dram"])
```

```python
from contextlib import ExitStack

import concourse.bass as bass
import numpy as np
from concourse import mybir

F32 = mybir.dt.float32
F32R = mybir.dt.float32r
BF16 = mybir.dt.bfloat16
I32 = mybir.dt.int32
ALU = mybir.AluOpType
ACT = mybir.ActivationFunctionType
X = mybir.AxisListType.X

P = 128
HD = 64
NEG = -1e30
BIG = 1e4
EPS = 1e-6


def nth(keys):
    return {k: n + 1 for n, k in enumerate(keys)}


def hybrid_block(nc, A, out, scratch):
    _, S, D = A["x"].shape
    FF = A["w_gate"].shape[2]
    NT, KT, FT = S // P, D // P, FF // P
    HALF, HT = S // 2, S // 2 // P
    H, KV, G = 8, 2, 4
    IH = 4
    TOPK = 256
    WIN = 512
    SLC, NSLC, TOPN = 64, S // 64, 8
    CSTR, CBLK = 16, 32
    NW = (S - CBLK) // CSTR + 1
    JP = CBLK // 2
    HH = A["cmp_w1_k"].shape[2] // P

    off = np.cumsum([0, 512, 128, 128, 128, 128, 128, 128, 24, 512, 64, 64, 256, 64, 4]).tolist()
    (_, o_kc, _, _, _, o_kwn, _, _, o_qb, o_kb, _, _, _, _, o_gm) = off
    IDX, QB, CMP, WKV, QA = "idx", "qb", "cmp", "win", "qa"
    ORDER = [IDX, QB, CMP, WKV, QA]
    COLS = {IDX: (o_kb, o_gm - o_kb), QB: (o_qb, 512), CMP: (o_kc, 512), WKV: (o_kwn, 280), QA: (0, 512)}
    ROPED = {IDX: [(0, 1), (128, 5)], QB: [(0, 8)], CMP: [(0, 2), (256, 2)], WKV: [(0, 2)], QA: [(0, 8)]}
    QBLK = {IDX: [(128, 4, 2)], QB: [(0, 8, 0)], CMP: [], WKV: [], QA: [(0, 8, 0)]}
    KBLK = {IDX: [(0, 0), (384, 6)], QB: [], CMP: [(256, 0), (320, 2)], WKV: [(0, 0), (64, 2)], QA: []}
    GROUPS = {IDX: [4, 4], QB: [4, 4], CMP: [4, 2], WKV: [4], QA: [4, 4]}

    x_rows = A["x"][0].rearrange("(i p) d -> i p d", p=P)
    out_rows = out[0].rearrange("(i p) d -> i p d", p=P)
    w_in = A["w_in"][0].rearrange("(k p) c -> p k c", p=P)

    ctx = ExitStack()

    def sem(name):
        return ctx.enter_context(nc.semaphore(name))

    def sb(stack, name, shape, dt=F32):
        return stack.enter_context(nc.sbuf_tensor(name, shape, dt))

    base, mix = ExitStack(), ExitStack()
    ident = sb(base, "ident", [P, P])
    stat = sb(base, "stat", [P, 5, 8])
    hstat = sb(base, "h_stat", [P, 2, 5, NT])
    kbT = sb(mix, "kbT", [P, 2, S], F32R)
    v_b = sb(mix, "v_b", [P, NT, HD])
    TK = list(range(TOPK // P, NT))
    sc_at = {i: sum(P * (m + 1) for m in TK if m < i) for i in TK}
    score = sb(mix, "score", [P, sum(P * (i + 1) for i in TK)])
    causal = sb(mix, "causal_bias", [P, S], BF16)
    winb = sb(mix, "window_bias", [P, WIN + P], BF16)
    cmpb = sb(mix, "cmp_bias", [P, NT, 64])
    v_slc = sb(mix, "v_slc", [P, NT, KV * HD])
    v_win = sb(mix, "v_win", [P, NT, KV * HD])
    nsa_gate = sb(mix, "nsa_gate", [P, NT, 3 * H])
    iw = sb(mix, "iw", [P, NT, IH])
    bit_cur = sb(mix, "bit_cur", [P, 8], I32)
    bit_flip = sb(mix, "bit_flip", [P, 8], I32)
    bit_try = sb(mix, "bit_try", [P, 8], I32)
    bit_keep = sb(mix, "bit_keep", [P, 8], I32)
    count = sb(mix, "count", [P, 8])
    need = sb(mix, "need", [P, 8])
    with ExitStack() as s:
        kcvcT = sb(s, "kcvcT", [P, 2, S])
    slcb = sb(mix, "slc_bias", [P, KV, S])

    def score_of(i):
        return score[:, sc_at[i]:sc_at[i] + P * (i + 1)]

    one = ExitStack()
    xTh = sb(one, "xTh", [P, KT, S], F32R)
    xTl = sb(one, "xTl", [P, KT, S], F32R)
    RAW, RING = 2, 4

    def ring_memory(stack, tag):
        raw = [sb(stack, f"{tag}_raw{n}", [P, 1024]) for n in range(RAW)]
        pairs = [[sb(stack, f"{tag}_{part}{n}", [P, 1024], F32R) for part in ("hi", "lo")] for n in range(RING)]
        return raw, [hi for hi, _ in pairs], [lo for _, lo in pairs]

    raw1, hi1, lo1 = ring_memory(one, "w1")
    zs = [sb(one, f"z{n}", [P, 512]) for n in range(2)]
    rot = sb(one, "rotated", [P, 512])
    ro = [sb(one, f"roped{n}", [P, 512]) for n in range(2)]
    blk = [sb(one, f"blocks{n}", [P, 8, P], F32R) for n in range(2)]
    kcvc = [sb(one, f"kcvc{n}", [P, 2 * P]) for n in range(2)]
    cosT = sb(one, "cosT", [P, NT, HD])
    sinT = sb(one, "sinT", [P, NT, HD])
    with ExitStack() as s:
        XR = 4
        xr = [sb(s, f"xr{n}", [P, D]) for n in range(XR)]
        xs = [sb(s, f"xs{n}", [P, D]) for n in range(2)]
        gain1 = sb(s, "gain_mix", [P, D])
    with ExitStack() as s:
        iqT = sb(s, "iqT", [P, IH, S], F32R)
        ikT = sb(s, "ikT", [P, 2, S], F32R)
    with ExitStack() as s:
        tq = [sb(s, f"turned{n}", [P, 8, P], F32R) for n in range(2)]
        gst = [sb(s, f"gate_out{n}", [P, 512]) for n in range(2)]
        tk_gt = sb(s, "above", [P, S])
        tk_eq = sb(s, "equal", [P, S])
        tk_cum = sb(s, "equal_so_far", [P, S])
    one.close()

    att = ExitStack()
    with ExitStack() as s:
        w2c = [sb(s, f"cmp_w2_{n}", [P, HH, 2, HD]) for n in "kv"]
        posc = [sb(s, f"cmp_pos_{n}", [P, CBLK]) for n in "kv"]
        xc = [sb(s, f"cmp_x_{n}", [P, JP, KV, 64]) for n in "kv"]
        hid_k = sb(s, "cmp_hid_k", [P, HH, KV * 64])
        hid_v = sb(s, "cmp_hid_v", [P, HH, KV, 2, 64])
    yTh, yTl = {}, {}
    for set_ in ("nsa", "dsa"):
        yTh[set_] = sb(att, f"yTh_{set_}", [P, KT // 2, S], F32R)
        yTl[set_] = sb(att, f"yTl_{set_}", [P, KT // 2, S], F32R)
    with ExitStack() as s:
        w1c = [sb(s, f"cmp_w1_{n}", [P, JP, HH * P]) for n in "kv"]
    kT = {a: sb(att, f"kT_{a}", [P, KV, 2, S], F32R) for a in ("slc", "win")}
    work = ExitStack()
    s_sb = [sb(work, f"s{n}", [P, S]) for n in range(2)]
    qt = [sb(work, f"q{n}", [P, H, P], F32R) for n in range(2)]
    kcm = sb(work, "k_cmp", [P, KV, 2, 64], F32R)
    vbd = sb(work, "v_cmp", [P, KV, P])
    PR = 3
    p_sb = [sb(work, f"p{n}", [P, S]) for n in range(PR)]
    pT = [sb(work, f"pT{n}", [P, NT, P]) for n in range(2)]
    ya = [sb(work, f"ya{n}", [P, H * HD]) for n in range(2)]
    yt = sb(work, "ytmp", [P, H * HD])
    c_s = sb(work, "c_s", [P, H, 64])
    c_p = sb(work, "c_p", [P, H, 64])
    c_pT = sb(work, "c_pT", [P, 4, P])
    c_st = sb(work, "c_st", [P, 4, H])
    pg = sb(work, "p_group", [P, KV, 68])
    bs = sb(work, "blk_score", [P, KV, NSLC])
    rk = sb(work, "rank", [P, KV, NSLC])
    cmp_a = sb(work, "cmp_above", [P, KV, NSLC, NSLC])
    cmp_b = sb(work, "cmp_equal", [P, KV, NSLC, NSLC])
    free_blk = sb(work, "blk_free", [P, NT, NSLC])
    set_blk = sb(work, "blk_set", [P, NT, NSLC])
    seen = sb(work, "row_sees_window", [P, 1])
    lower = sb(work, "lower_index", [P, NSLC, NSLC])
    nmax = sb(work, "nmax", [P, 3, NT, H])
    psum_p = sb(work, "psum_p", [P, 3, NT, H])
    psum_r = sb(work, "psum_r", [P, 3, NT, H])
    work.close()
    att.close()
    mix.close()

    late = ExitStack()
    raw2, hi2, lo2 = ring_memory(late, "w2")
    hrow = sb(late, "h", [P, NT, D])
    with ExitStack() as s:
        sb(s, "skip_y", [P, 11 * S])
        mTh = sb(s, "mTh", [P, KT, S], F32R)
        mTl = sb(s, "mTl", [P, KT, S], F32R)
        gl = [sb(s, f"gates{n}", [P, 2, HALF]) for n in range(2)]
        with ExitStack() as s7:
            ma = sb(s7, "ma", [P, HALF])
            mb = sb(s7, "mb", [P, HALF])
        squares = sb(s, "squares", [P, D])
        mf = [sb(s, f"merged{n}", [P, HALF]) for n in range(2)]
        xl = [gl[n][:, 0, :] for n in range(2)]
    hTh = sb(late, "hTh", [P, KT, HALF], F32R)
    hTl = sb(late, "hTl", [P, KT, HALF], F32R)
    aTh = sb(late, "aTh", [P, FT, HALF], F32R)
    aTl = sb(late, "aTl", [P, FT, HALF], F32R)
    with ExitStack() as s:
        sg = [sb(s, f"silu{n}", [P, HALF]) for n in range(2)]
        af = [sb(s, f"act{n}", [P, HALF]) for n in range(2)]
    hn = [sb(late, f"hn{n}", [P, D]) for n in range(2)]
    gain2 = sb(late, "gain2", [P, D])
    late.close()
    base.close()

    psA = ctx.enter_context(nc.psum_tensor("psA", [P, 4, 512], F32))
    psT = ctx.enter_context(nc.psum_tensor("psT", [P, 4, 512], F32))
    psA2, psT2 = (ps[:].rearrange("p (a b) c -> p a (b c)", a=2) for ps in (psA, psT))
    TURN_AT = [12, 13, 14, 14]
    OUT_AT = 6

    def chunk_items(src, first, width):
        return [[(src[:, 2 * n:2 * n + 2, first:first + width], 0, 2, width)] for n in range(KT // 2)]

    items1 = sum((chunk_items(w_in, *COLS[c]) for c in ORDER), [])
    NCH = len(items1)
    items1 += [[(w_in[:, :, o_gm + P * j:o_gm + P * (j + 1)], 0, KT, P)] for j in range(2 * KT)]
    wa = A["w_branch_nsa"][0].rearrange("(k p) c -> p k c", p=P)
    wb = A["w_branch_dsa"][0].rearrange("(k p) c -> p k c", p=P)
    wo = A["w_out"][0].rearrange("(k p) c -> p k c", p=P)
    wg = A["w_gate"][0].rearrange("(k p) c -> p k c", p=P)
    wu = A["w_up"][0].rearrange("(k p) c -> p k c", p=P)
    wd = A["w_down"][0].rearrange("(k p) c -> p k c", p=P)
    items2 = [[(w[:, :, P * j:P * (j + 1)], 512 * n, KT // 2, P) for n, w in enumerate((wa, wb))]
              for j in range(KT)]
    items2 += sum((chunk_items(wo, 512 * n, 512) for n in range(2)), [])
    for t in range(2):
        for f in range(FT):
            items2 += [[(w[:, :, P * f:P * (f + 1)], 0, KT, P)] for w in (wg, wu)]
        for n in range(2):
            items2 += [[(wd[:, 2 * a:2 * a + 2, 512 * n:512 * (n + 1)], 0, 2, 512)] for a in range(FT // 2)]
    Z_STEPS, G_STEPS = 8 * len(ORDER), 4 * KT
    free1 = [8 * (n // 4) + 7 if n < NCH else Z_STEPS + 2 * (n - NCH) + 1 for n in range(len(items1))]
    M_STEPS, O_STEPS, F_STEPS = 2 * KT, 2 * NT, FT
    free2 = [2 * j + 1 for j in range(KT)] + [M_STEPS + 8 * (n // 4) + 7 for n in range(8)]
    for t in range(2):
        at = M_STEPS + O_STEPS + 2 * F_STEPS * t
        free2 += [at + n // 2 for n in range(2 * FT)] + [at + FT + n for n in range(FT)]

    class Ring:

        def __init__(self, tag, items, free, raw, hi, lo):
            self.items, self.free, self.raw, self.hi, self.lo = items, free, raw, hi, lo
            self.gone = []
            self.raw_in = [sem(f"{tag}_raw_in{n}") for n in range(RAW)]
            self.hi_done, self.lo_done, self.freed = sem(f"{tag}_hi"), sem(f"{tag}_lo"), sem(f"{tag}_free")
            self.landed, total = [], [0] * RAW
            for n, parts in enumerate(items):
                total[n % RAW] += 16 * len(parts)
                self.landed.append(total[n % RAW])

        def due(self, step, depth):
            return [n for n in range(depth, len(self.items)) if self.free[n - depth] == step]

        def used(self, n):
            parts = self.items[n]
            return parts[-1][1] + parts[-1][2] * parts[-1][3]

        def load(self, sp, n):
            if n >= RAW:
                sp.wait_ge(self.lo_done, n - RAW + 1)
            for src, at, k, w in self.items[n]:
                dst = self.raw[n % RAW][:, at:at + k * w].rearrange("p (k w) -> p k w", k=k)
                sp.dma_start(dst, src).then_inc(self.raw_in[n % RAW], 16)

        def split_hi(self, act, n):
            act.wait_ge(self.raw_in[n % RAW], self.landed[n])
            if n >= RING:
                act.wait_ge(*self.gone[n - RING])
            u = self.used(n)
            nc.scalar.copy(self.hi[n % RING][:, 0:u], self.raw[n % RAW][:, 0:u]).then_inc(self.hi_done, 1)

        def split_lo(self, pool, n):
            pool.wait_ge(self.hi_done, n + 1)
            u = self.used(n)
            nc.gpsimd.tensor_tensor(self.lo[n % RING][:, 0:u], self.raw[n % RAW][:, 0:u],
                                    self.hi[n % RING][:, 0:u].bitcast(F32), ALU.subtract).then_inc(self.lo_done, 1)

        def parts(self, n, k):
            return tuple(x[n % RING][:, 0:self.used(n)].rearrange("p (k w) -> p k w", k=k)
                         for x in (self.hi, self.lo))

    w1 = Ring("w1", items1, free1, raw1, hi1, lo1)
    w2 = Ring("w2", items2, free2, raw2, hi2, lo2)

    zsteps = [(c, i) for c in ORDER for i in range(NT)]
    turned = nth([(q, g) for q, (c, i) in enumerate(zsteps) for g in range(len(GROUPS[c]))])
    spills = nth([q for q, (c, i) in enumerate(zsteps) if c != IDX])
    cmps = nth([q for q, (c, i) in enumerate(zsteps) if c == CMP])
    NA = 2 * NT
    LAST = len(zsteps) - 1
    iunits = [(i, h) for i in TK for h in range(IH)]

    units = [("dsa", i, h) for i in range(NT) for h in range(H)]
    ND = len(units)
    for i in range(NT):
        units += [("win", i, h) for h in range(H)] + [("slc", i, h) for h in range(H)]
    CH_AT, CK_AT = 32, 34
    W2_AT = [ND + 64, ND + 72]
    BR = {"slc": 0, "win": 1, "dsa": 2}

    def keys_of(a, i):
        n = min(i + 1, WIN // P + 1) if a == "win" else i + 1
        return i + 1 - n, n

    def seg(n):
        return [(c, min(c + 512, n * P)) for c in range(0, n * P, 512)]

    E_LAG, T_LAG, V_LAG, F_LAG, Y_LAG = 1, 2, 3, 4, 6
    STEPS6 = len(units) + Y_LAG + 2
    C_BIAS, C_MAX, C_EXP, C_SUM, C_RECIP, C_TURN, C_RANK, C_OUT = 1, 2, 4, 5, 6, 8, 8, 9

    def at(u):
        return units[u] if 0 <= u < len(units) else (None, None, None)

    def cmp_tile(u, stage):
        for i in range(NT):
            if u - stage == ND + 16 * i - 6:
                return i
        return None

    def y_of(u):
        a, i, h = at(u - Y_LAG)
        return (a, i) if a in ("slc", "dsa") and h == H - 1 else None

    groups6, opened = [], []
    for u in range(STEPS6):
        a, i, h = at(u - T_LAG)
        if a:
            groups6 += [("p", u - T_LAG, g) for g in range(len(seg(keys_of(a, i)[1])))]
        a, i, h = at(u - V_LAG)
        if a and h == 0:
            opened.append((a, i))
        if u == CH_AT:
            groups6.append(("ch", 0, 0))
        if u == CK_AT:
            groups6.append(("ck", 0, 0))
        for key, stage in (("cs", 0), ("cp", C_TURN), ("co", C_OUT)):
            if cmp_tile(u, stage) is not None:
                groups6.append((key, cmp_tile(u, stage), 0))
        if y_of(u):
            groups6.append(("y", *y_of(u)))
    g6 = {k: n for n, k in enumerate(groups6)}
    o6 = {k: n for n, k in enumerate(opened)}

    def by_act(key):
        return key[0] in ("ch", "cp") or (key[0] == "p" and (key[1] + key[2]) % 2 == 0)

    act_took = nth([k for k in groups6 if by_act(k)])
    dve_took = nth([k for k in groups6 if not by_act(k)])
    o_took = nth(opened)
    ysteps = nth([k for k in groups6 if k[0] == "y"])
    groups_y = list(ysteps)

    consts = sem("consts")
    x_in = [sem(f"x_in{n}") for n in range(XR)]
    table_in = sem("table_in")
    sq_done, var_done, sd_done, xs_done = sem("sq"), sem("var"), sem("sd"), sem("xs")
    xt_ps, xh_done, xl_done = sem("xt_ps"), sem("xh"), sem("xl")
    z_ps, z_out, rope_done = sem("z_ps"), sem("z_out"), sem("rope")
    bh_done, bl_done = sem("blk_hi"), sem("blk_lo")
    zt_ps, zt_out = sem("zt_ps"), sem("zt_out")
    spilled = [sem(f"spilled{n}") for n in range(2)]
    id_ps, relu_done, sc_done = sem("id_ps"), sem("relu"), sem("score_sum")
    g_ps, g_out = sem("g_ps"), sem("g_out")
    g_stored = [sem(f"g_stored{n}") for n in range(2)]
    bs_done, rank_done = sem("blk_score_done"), sem("rank_done")
    dve_seq, pool_seq = sem("dve_seq"), sem("pool_seq")
    tk_done = sem("topk_bias")
    cw_in, pos_in, cx_k, cx_v = sem("cw_in"), sem("pos_in"), sem("cx_k"), sem("cx_v")
    ck_hi = sem("ck_hi")
    kT_in = sem("kT_in")
    q_in = [sem(f"q_in{n}") for n in range(2)]
    s_ps, s_done, p_done = sem("s_ps"), sem("s_done"), sem("p_done")
    t_ps, t_act, t_dve = sem("t_ps"), sem("t_act"), sem("t_dve")
    cm_done, cs_out, cr_done, ce_done, cp_done, sb_done = sem("cmp_max"), sem("cs_out"), sem("cmp_recip"), sem("ce"), sem("cp"), sem("slc_bias_done")
    pv_ps, o_out, y_done, yh_done = sem("pv_ps"), sem("o_out"), sem("y_added"), sem("yh")
    gl_in = [sem(f"gl_in{n}") for n in range(2)]
    m_ps, m_done, mh_done, ml_done = sem("m_ps"), sem("m_done"), sem("mh"), sem("ml")
    xl_in = [sem(f"xl_in{n}") for n in range(2)]
    o_ps, h_done = sem("o_ps"), sem("h_done")
    gain_in = sem("gain_in")
    hq_done, hv_done, hd_done, hn_done = sem("hq"), sem("hv"), sem("hd"), sem("hn_done")
    ht_ps, hh_done, hl_done = sem("ht_ps"), sem("hh"), sem("hl")
    f_ps, sg_done, af_done, ah_done, al_done = sem("f_ps"), sem("sg"), sem("af"), sem("ah"), sem("al")
    d_ps, d_done, out_ready, stored = sem("d_ps"), sem("d_done"), sem("out_ready"), sem("stored")

    qD = {"nsa": scratch["q_nsa"], "dsa": scratch["q_dsa"]}
    kD = {"slc": scratch["k_slc"], "win": scratch["k_win"]}
    gD = scratch["gates"]

    for n in range(len(items1)):
        if n < NCH:
            ch, a = n // 4, n % 4
            w1.gone.append((w1.freed, 3 * ch + a + 1) if a < 3 else (z_ps, 8 * ch + 8))
        else:
            w1.gone.append((g_ps, 2 * (n - NCH) + 2))
    w2.gone = [(m_ps, 2 * j + 2) for j in range(KT)]
    frees = 0
    for n in range(2):
        w2.gone += [(w2.freed, frees + 1), (w2.freed, frees + 2), (w2.freed, frees + 3), (o_ps, NT * (n + 1))]
        frees += 3
    for t in range(2):
        for f in range(FT):
            w2.gone += [(f_ps, FT * t + f + 1)] * 2
        for n in range(2):
            w2.gone += [(w2.freed, frees + a + 1) for a in range(FT // 2 - 1)] + [(d_ps, 8 * t + 4 * n + 4)]
            frees += FT // 2 - 1

    block = ctx.enter_context(nc.Block())

    def tok(i):
        return slice(P * i, P * (i + 1))

    def heads(ap, n):
        return ap.rearrange("p (h d) -> p h d", h=n)

    N_CONST1 = 9
    N_CONST6 = N_CONST1 + 2 + 11

    def windows(eng, n, done):
        for g in range(KV):
            src = kcvcT[HD * g:HD * (g + 1), n, :].rearrange("p (c s) -> p s c", s=CSTR)
            for u in range(2):
                for j in range(2):
                    last = eng.tensor_tensor(
                        xc[n][HD * u:HD * (u + 1), 8 * j:8 * j + 8, g, 0:NW], src[:, u::2, j:j + NW],
                        posc[n][HD * g:HD * (g + 1), CSTR * j + u:CSTR * (j + 1):2].unsqueeze(2).to_broadcast([HD, 8, NW]),
                        ALU.add)
                    last.then_inc(done, 1)

    def evac_p(eng, copy, v, act_side):
        a, i, h = at(v)
        for g, (c0, c1) in enumerate(seg(keys_of(a, i)[1])):
            key = ("p", v, g)
            if by_act(key) != act_side:
                continue
            eng.wait_ge(t_ps, g6[key] + 1)
            if v >= 2:
                eng.wait_ge(pv_ps, v - 1)
            copy(pT[v % 2][:, c0 // P:c1 // P, :].rearrange("p k t -> p (k t)"), psT[:, g6[key] % 2, 0:c1 - c0])\
                .then_inc(t_act if act_side else t_dve, 1)

    @block.sync
    def _(sp):
        def load_x(i):
            if i >= XR:
                sp.wait_ge(xs_done, i - XR + 1)
            sp.dma_start(xr[i % XR][:], x_rows[i]).then_inc(x_in[i % XR], 16)

        for i in range(XR):
            load_x(i)
        sp.dma_start(gain1[:], A["norm_mix"][0:1, :].to_broadcast([P, D])).then_inc(gain_in, 16)
        for n in range(RAW):
            w1.load(sp, n)
        sp.dma_start(cosT[:], A["rope_cos"].rearrange("(i p) d -> p i d", p=P)).then_inc(table_in, 16)
        sp.dma_start(sinT[:], A["rope_sin"].rearrange("(i p) d -> p i d", p=P)).then_inc(table_in, 16)
        for i in range(XR, NT):
            load_x(i)
        for n in range(RAW, RAW + RING):
            w1.load(sp, n)

        def spill(q):
            c, i = zsteps[q]
            if c == IDX:
                return
            sp.wait_ge(zt_out, turned[q, 0] if c in (CMP, WKV) else turned[q, 1])
            n = spills[q] - 1
            t = tq[n % 2]
            if c in (QA, QB):
                dst, src = qD["nsa" if c == QA else "dsa"][i], t[:].rearrange("p b t -> p (b t)")
            else:
                dst, src = kD["slc" if c == CMP else "win"][:, :, tok(i)], t[:, 0:4, :]
            sp.dma_start(dst, src.bitcast(F32)).then_inc(spilled[n % 2], 16)

        for q in range(Z_STEPS + 3):
            if q < Z_STEPS:
                for n in w1.due(q, RAW + RING):
                    w1.load(sp, n)
            if q >= 3:
                spill(q - 3)
        def load_q(k):
            set_, i = ("dsa", k) if k < NT else ("nsa", k - NT)
            if k >= 2:
                sp.wait_ge(s_ps, 8 * (k - 1) if k <= NT + 1 else ND + 16 * (k - 1 - NT))
            sp.dma_start(qt[k % 2][:].rearrange("p h t -> p (h t)").bitcast(F32), qD[set_][i])\
                .then_inc(q_in[k % 2], 16)

        def first_queries():
            for n in range(2):
                sp.wait_ge(spilled[n], 16 * len([s for s in spills.values() if (s - 1) % 2 == n]))
            load_q(0)
            load_q(1)

        for g in range(G_STEPS):
            for n in w1.due(Z_STEPS + g, RAW + RING):
                w1.load(sp, n)
            if g == 4:
                sp.wait_ge(zt_ps, len(turned))
                first_queries()
            sp.wait_ge(g_out, g + 1)
            sp.dma_start(gD[g // 2, :, HALF * (g % 2):HALF * (g % 2 + 1)], gst[g % 2][:])\
                .then_inc(g_stored[g % 2], 16)

        sp.wait_ge(g_ps, G_STEPS)
        for n, kv in enumerate("kv"):
            for r in range(2):
                sp.dma_start(posc[n][HD * r:HD * (r + 1), :], A[f"cmp_pos_{kv}"][0].rearrange("j d -> d j"),
                             allow_slow_non_contiguous=True).then_inc(pos_in, 16)
        for n, kv in enumerate("kv"):
            sp.dma_start(w1c[n][:], A[f"cmp_w1_{kv}"][0].rearrange("(j p) c -> p j c", p=P)).then_inc(cw_in, 16)
            for r in range(2):
                sp.dma_start(w2c[n][:, :, r, :], A[f"cmp_w2_{kv}"][0].rearrange("(a p) d -> p a d", p=P))\
                    .then_inc(cw_in, 16)
        for k in range(2, 2 * NT):
            load_q(k)
            if k == CK_AT // 8 + 1:
                sp.wait_ge(t_dve, dve_took["ck", 0, 0])
                for a in ("win", "slc"):
                    sp.dma_start(kT[a][:].rearrange("p a b s -> p (a b) s").bitcast(F32), kD[a]).then_inc(kT_in, 16)
            if k == NT + 3:
                sp.wait_ge(s_done, ND)
                sp.wait_ge(pv_ps, ND)
                w2.load(sp, 0)
                w2.load(sp, 1)
            if k == 2 * NT - 1:
                w2.load(sp, 2)
                w2.load(sp, 3)

        sp.wait_ge(pv_ps, len(units))
        sp.wait_ge(t_dve, len(dve_took))
        for n in range(2):
            sp.wait_ge(g_stored[n], 16 * (G_STEPS // 2))
        for n in range(2 * RAW, RAW + RING):
            w2.load(sp, n)
        sp.dma_start(gain2[:], A["norm_ffn"][0:1, :].to_broadcast([P, D])).then_inc(gain_in, 16)
        for m in range(M_STEPS):
            for n in w2.due(m - 2, RAW + RING):
                w2.load(sp, n)
            if m >= 2:
                sp.wait_ge(m_done, m - 1)
            j, half = m // 2, m % 2
            for b in range(2):
                sp.dma_start(gl[m % 2][:, b, :], gD[KT * b + j, :, HALF * half:HALF * (half + 1)])\
                    .then_inc(gl_in[m % 2], 16)
        sp.wait_ge(m_done, M_STEPS)
        for o in range(O_STEPS + 2):
            for n in w2.due(M_STEPS + o - 2, RAW + RING):
                w2.load(sp, n)
            if o >= O_STEPS:
                continue
            if o >= 2:
                sp.wait_ge(h_done, o - 1)
            n, i = o // NT, o % NT
            sp.dma_start(xl[o % 2], x_rows[i][:, 512 * n:512 * (n + 1)]).then_inc(xl_in[o % 2], 16)
        def store(i):
            sp.wait_ge(out_ready, i + 1)
            sp.dma_start(out_rows[i], hrow[:, i, :]).then_inc(stored, 16)

        for t in range(2):
            at_ = M_STEPS + O_STEPS + 2 * FT * t
            for f in range(FT):
                for n in w2.due(at_ + f, RAW + RING):
                    w2.load(sp, n)
                if t == 1 and OUT_AT <= f - 1 < OUT_AT + HT:
                    store(f - 1 - OUT_AT)
            for a in range(FT):
                for n in w2.due(at_ + FT + a, RAW + RING):
                    w2.load(sp, n)
                if t == 0 and a == FT // 2 - 1:
                    sp.wait_ge(hn_done, NT)
                    sp.dma_start(gain2[:], A["norm_final"].rearrange("(a d) -> a d", a=1).to_broadcast([P, D]))\
                        .then_inc(gain_in, 16)
        for i in range(HT, NT):
            store(i)
        sp.wait_ge(stored, 16 * NT)

    @block.gpsimd
    def _(pool):
        total = [0]

        def made(ins):
            ins.then_inc(consts, 1)
            total[0] += 1
            pool.wait_ge(consts, total[0])

        def select(ap, keep, fill, first, per_row, pattern):
            made(pool.affine_select(out=ap, in_=ap, compare_op=keep, fill=fill, base=first,
                                    pattern=pattern, channel_multiplier=per_row))

        made(pool.memset(ident[:], 0.0))
        select(ident[:], ALU.not_equal, 1.0, 0, 1, [[-1, P]])
        made(pool.memset(causal[:], 0.0))
        select(causal[:, S - P:S], ALU.is_ge, NEG, 0, 1, [[-1, P]])
        made(pool.memset(winb[:], 0.0))
        select(winb[:, WIN:WIN + P], ALU.is_ge, NEG, 0, 1, [[-1, P]])
        select(winb[:, 0:P], ALU.is_gt, NEG, 0, -1, [[1, P]])
        made(pool.memset(cmpb[:], 0.0))
        select(cmpb[:], ALU.is_ge, NEG, 1 - CBLK, 1, [[P, NT], [-CSTR, 64]])
        for n in range(len(items1)):
            w1.split_lo(pool, n)
        pool.wait_ge(g_ps, G_STEPS)
        pool.wait_ge(pos_in, 16 * 4)
        pool.wait_ge(zt_out, len(turned))
        for n, done in ((0, cx_k), (1, cx_v)):
            made(pool.memset(xc[n][:, :, :, NW:64], 0.0))
            windows(nc.gpsimd, n, done)
            pool.wait_ge(done, 8)
        pool.wait_ge(tk_done, len(TK))
        made(pool.memset(lower[:], 1.0))
        select(lower[:], ALU.is_gt, 0.0, 0, 0, [[1, NSLC], [-1, NSLC]])
        made(pool.memset(free_blk[:], 1.0))
        select(free_blk[:], ALU.is_ge, 0.0, -2 * SLC, 1, [[P, NT], [-SLC, NSLC]])
        made(pool.memset(free_blk[:, :, 0:1], 0.0))
        made(pool.memset(set_blk[:], BIG))
        select(set_blk[:], ALU.is_ge, NEG, 0, 1, [[P, NT], [-SLC, NSLC]])
        select(set_blk[:, :, 1:NSLC], ALU.is_gt, 0.0, 3 * SLC, -1, [[-P, NT], [SLC, NSLC - 1]])
        made(pool.memset(pg[:], 0.0))
        made(pool.memset(seen[:], 1.0))
        select(seen[:], ALU.is_ge, 0.0, 1 - CBLK, 1, [[0, 1]])
        seq = [0]

        def then(ins):
            ins.then_inc(pool_seq, 1)
            seq[0] += 1
            pool.wait_ge(pool_seq, seq[0])

        def block_scores(i):
            head = c_p[:].rearrange("p (a g) w -> p g a w", a=KV)
            then(nc.gpsimd.tensor_tensor(pg[:, :, 1:65], head[:, 0], head[:, 1], ALU.add))
            for g in range(2, G):
                then(nc.gpsimd.tensor_tensor(pg[:, :, 1:65], pg[:, :, 1:65], head[:, g], ALU.add))
            then(nc.gpsimd.tensor_tensor(bs[:], pg[:, :, 0:64:4], pg[:, :, 1:65:4], ALU.add))
            for k in (2, 3, 4):
                then(nc.gpsimd.tensor_tensor(bs[:], bs[:], pg[:, :, k:k + 64:4], ALU.add))
            then(nc.gpsimd.tensor_tensor(bs[:], bs[:], free_blk[:, i, :].unsqueeze(1).to_broadcast([P, KV, NSLC]), ALU.mult))
            nc.gpsimd.tensor_tensor(bs[:], bs[:], set_blk[:, i, :].unsqueeze(1).to_broadcast([P, KV, NSLC]), ALU.add)\
                .then_inc(bs_done, 1)

        def block_bias(i):
            n, w = 2 * (i + 1), P * (i + 1)
            pool.wait_ge(rank_done, i - TOPN // 2 + 1)
            pool.wait_ge(s_done, ND + 16 * i)
            for a in range(KV):
                last = nc.gpsimd.tensor_copy(slcb[:, a, 0:w].rearrange("p (j s) -> p j s", s=SLC),
                                      rk[:, a, 0:n].unsqueeze(2).to_broadcast([P, n, SLC]))
            then(last)
            for a in range(KV):
                last = nc.gpsimd.tensor_tensor(slcb[:, a, w - P:w], slcb[:, a, w - P:w], causal[:, S - P:S], ALU.add)
            last.then_inc(sb_done, 1)

        for u in range(STEPS6):
            i = cmp_tile(u, C_MAX)
            if i is not None:
                pool.wait_ge(cm_done, i + 1)
                nc.gpsimd.tensor_tensor(c_s[:], c_s[:], c_st[:, 0, :].unsqueeze(2).to_broadcast([P, H, 64]), ALU.subtract)\
                    .then_inc(cs_out, 1)
            i = cmp_tile(u, C_RECIP)
            if i is not None:
                pool.wait_ge(cr_done, i + 1)
                nc.gpsimd.tensor_tensor(c_p[:], c_p[:], c_st[:, 2, :].unsqueeze(2).to_broadcast([P, H, 64]), ALU.mult)\
                    .then_inc(cp_done, 1)
                if i >= TOPN // 2:
                    pool.wait_ge(cp_done, i + 1)
                    block_scores(i)
            i = cmp_tile(u, C_RANK)
            if i is not None and i >= TOPN // 2:
                block_bias(i)
            a, i, h = at(u - F_LAG)
            if a in ("win", "slc") and h == H - 1:
                y = ya[(ysteps["y", "slc", i] - 1) % 2]
                pool.wait_ge(o_out, o_took[a, i])
                if o_took[a, i] > NT + 1:
                    pool.wait_ge(y_done, o_took[a, i] - NT - 1)
                pool.wait_ge(t_dve, dve_took["co", i, 0])
                nc.gpsimd.tensor_tensor(y[:], y[:], yt[:], ALU.add).then_inc(y_done, 1)
            if u in W2_AT:
                w2.split_lo(pool, W2_AT.index(u))
        for n in range(len(W2_AT), len(items2)):
            w2.split_lo(pool, n)

    @block.scalar
    def _(act):
        a_ = nc.scalar

        for b in range(2):
            for i in range(HT * b, HT * (b + 1)):
                act.wait_ge(x_in[i % XR], 16 * (i // XR + 1))
                if i >= 2:
                    act.wait_ge(sq_done, i - 1)
                a_.activation(blk[i % 2][:].rearrange("p b t -> p (b t)").bitcast(F32), xr[i % XR][:], ACT.Square,
                              accum_out=stat[:, 0, i:i + 1]).then_inc(sq_done, 1)
            act.wait_ge(var_done, b + 1)
            a_.activation(stat[:, 2, HT * b:HT * b + HT], stat[:, 1, HT * b:HT * b + HT], ACT.Sqrt).then_inc(sd_done, 1)
            for n in range(8 * b, 8 * b + 8):
                i, g = n // 2, n % 2
                act.wait_ge(xt_ps, n + 1)
                a_.copy(xTh[:, 4 * g:4 * g + 4, tok(i)], psT[:, n % 4, :].rearrange("p (k t) -> p k t", k=4))\
                    .then_inc(xh_done, 1)
            for n in (2 * b, 2 * b + 1):
                w1.split_hi(act, n)

        def z_evac(q):
            c, i = zsteps[q]
            ps = psA[:, q % 4, :]
            act.wait_ge(z_ps, q + 1)
            if q >= 2:
                act.wait_ge(rope_done, q - 1)
            if c == IDX:
                a_.copy(zs[q % 2][:, 0:448], ps[:, 0:448])
                a_.copy(v_b[:, i, :], ps[:, 64:128])
                last = a_.activation(iw[:, i, :], ps[:, 448:452], ACT.Copy, scale=IH ** -0.5)
            elif c == CMP:
                a_.copy(zs[q % 2][:, 0:384], ps[:, 0:384])
                a_.copy(v_slc[:, i, :], ps[:, 384:512])
                if cmps[q] > 2:
                    act.wait_ge(zt_ps, turned[q - 2, 1])
                last = a_.copy(kcvc[q % 2][:, P:2 * P], ps[:, P:2 * P])
            elif c == WKV:
                a_.copy(zs[q % 2][:, 0:128], ps[:, 0:128])
                a_.copy(v_win[:, i, :], ps[:, 128:256])
                last = a_.activation(nsa_gate[:, i, :], ps[:, 256:280], ACT.Sigmoid)
            else:
                last = a_.copy(zs[q % 2][:], ps)
            last.then_inc(z_out, 1)

        def block_hi(q):
            c, i = zsteps[q]
            act.wait_ge(rope_done, q + 1)
            if q >= 2:
                act.wait_ge(zt_ps, turned[q - 2, len(GROUPS[zsteps[q - 2][0]]) - 1])
            else:
                act.wait_ge(sq_done, NT)
            r, t = ro[q % 2], blk[q % 2]
            for col, n, b in QBLK[c]:
                last = a_.copy(t[:, b:b + n, 0:HD], heads(r[:, col:col + n * HD], n))
            for col, b in KBLK[c]:
                last = a_.copy(t[:, b, :].rearrange("p (r d) -> p r d", r=2),
                               r[:, col:col + HD].unsqueeze(1).to_broadcast([P, 2, HD]))
            last.then_inc(bh_done, 1)

        def turned_out(q):
            c, i = zsteps[q]
            for g, n in enumerate(GROUPS[c]):
                k = turned[q, g]
                ps = psT[:, (NA + k - 1) % 4, :].rearrange("p (b t) -> p b t", b=4)
                if q == 0 and g == 0:
                    act.wait_ge(xt_ps, NA)
                    act.wait_ge(xs_done, NT)
                act.wait_ge(zt_ps, k)
                if c == IDX and g == 0:
                    a_.copy(kbT[:, :, tok(i)], ps[:, 0:2, :])
                    last = a_.copy(iqT[:, 0:2, tok(i)], ps[:, 2:4, :])
                elif c == IDX:
                    a_.copy(iqT[:, 2:4, tok(i)], ps[:, 0:2, :])
                    last = a_.copy(ikT[:, :, tok(i)], ps[:, 2:4, :])
                elif c == CMP and g == 1:
                    last = a_.copy(kcvcT[:, :, tok(i)], ps[:, 0:2, :])
                else:
                    s_ = spills[q] - 1
                    if s_ >= 2 and g == 0:
                        act.wait_ge(spilled[s_ % 2], 16 * (s_ // 2))
                    last = a_.copy(tq[s_ % 2][:, 4 * g:4 * g + 4, :], ps)
                last.then_inc(zt_out, 1)

        def stage2(first, stop):
            for q in range(first, stop + 2):
                if q < stop:
                    for n in w1.due(q, RING):
                        w1.split_hi(act, n)
                    z_evac(q)
                if first <= q - 1 < stop:
                    block_hi(q - 1)
                if first <= q - 2 < stop:
                    turned_out(q - 2)

        stage2(0, NT)
        for v, (i, h) in enumerate(iunits):
            act.wait_ge(id_ps, v + 1)
            ps = psA2[:, v % 2, 0:P * (i + 1)]
            a_.activation(ps, ps, ACT.Relu, scale=HD ** -0.5).then_inc(relu_done, 1)
        act.wait_ge(id_ps, len(iunits))
        stage2(NT, Z_STEPS)
        for g in range(G_STEPS):
            for n in w1.due(Z_STEPS + g, RING):
                w1.split_hi(act, n)
            act.wait_ge(g_ps, g + 1)
            if g >= 2:
                act.wait_ge(g_stored[g % 2], 16 * (g // 2))
            a_.activation(gst[g % 2][:], psA[:, g % 4, :], ACT.Sigmoid).then_inc(g_out, 1)

        for u in range(STEPS6):
            if u - 1 == CH_AT:
                act.wait_ge(t_ps, g6["ch", 0, 0] + 1)
                ps = psT[:, g6["ch", 0, 0] % 2, :].rearrange("p (n a g w) -> p n a g w", n=2, a=HH, g=KV)
                a_.activation(hid_k[:].rearrange("p a (g w) -> p a g w", g=KV), ps[:, 0], ACT.Gelu_apprx_tanh)
                for r in range(2):
                    last = a_.activation(hid_v[:, :, :, r, :], ps[:, 1], ACT.Gelu_apprx_tanh)
                last.then_inc(t_act, 1)
            if u - 1 == CK_AT:
                act.wait_ge(t_ps, g6["ck", 0, 0] + 1)
                a_.copy(kcm[:, :, 0, :], psT[:, g6["ck", 0, 0] % 2, 0:P].rearrange("p (g w) -> p g w", g=KV))\
                    .then_inc(ck_hi, 1)
            if u in W2_AT:
                w2.split_hi(act, W2_AT.index(u))
            i = cmp_tile(u - 1, C_TURN)
            if i is not None:
                act.wait_ge(t_ps, g6["cp", i, 0] + 1)
                if i >= 1:
                    act.wait_ge(t_ps, g6["co", i - 1, 0] + 1)
                a_.copy(c_pT[:].rearrange("p a t -> p (a t)"), psT[:, g6["cp", i, 0] % 2, :]).then_inc(t_act, 1)
            if y_of(u - 1):
                key = ("y", *y_of(u - 1))
                act.wait_ge(t_ps, g6[key] + 1)
                a_.copy(yTh["dsa" if key[1] == "dsa" else "nsa"][:, :, tok(key[2])],
                        psT[:, g6[key] % 2, :].rearrange("p (k t) -> p k t", k=4)).then_inc(yh_done, 1)
            v = u - E_LAG
            a, i, h = at(v)
            if a:
                n = P * keys_of(a, i)[1]
                act.wait_ge(s_done, v + 1)
                if v >= PR:
                    b, j, _ = at(v - PR)
                    act.wait_ge(t_ps, g6["p", v - PR, len(seg(keys_of(b, j)[1])) - 1] + 1)
                a_.activation(p_sb[v % PR][:, 0:n], s_sb[v % 2][:, 0:n], ACT.Exp, scale=-1.0,
                              bias=nmax[:, BR[a], i, h:h + 1],
                              accum_out=psum_p[:, BR[a], i, h:h + 1]).then_inc(p_done, 1)
            v = u - T_LAG
            if at(v)[0]:
                evac_p(act, a_.copy, v, True)
            i = cmp_tile(u, C_EXP)
            if i is not None:
                act.wait_ge(cs_out, i + 1)
                if i > TOPN // 2:
                    act.wait_ge(bs_done, i - TOPN // 2)
                a_.activation(c_p[:], c_s[:], ACT.Exp, scale=HD ** -0.5).then_inc(ce_done, 1)

        act.wait_ge(pv_ps, len(units))
        for n in range(len(W2_AT), RING):
            w2.split_hi(act, n)
        for m in range(M_STEPS):
            for n in w2.due(m, RING):
                w2.split_hi(act, n)
            act.wait_ge(m_done, m + 1)
            j, half = m // 2, m % 2
            a_.copy(mTh[:, j, HALF * half:HALF * (half + 1)], mf[m % 2][:]).then_inc(mh_done, 1)
        def squared(r, i, scratch):
            if r == 0 and i >= 1:
                act.wait_ge(hq_done, i)
            a_.activation(scratch, hrow[:, i, :], ACT.Square, accum_out=hstat[:, r, 0, i:i + 1]).then_inc(hq_done, 1)

        def root(r, c, n):
            act.wait_ge(hv_done, n)
            a_.activation(hstat[:, r, 2, c], hstat[:, r, 1, c], ACT.Sqrt).then_inc(hd_done, 1)

        def turned_h(i):
            b = i % HT
            for g in range(2):
                n = 2 * i + g
                act.wait_ge(ht_ps, n + 1)
                if n == 8:
                    act.wait_ge(f_ps, FT)
                a_.copy(hTh[:, 4 * g:4 * g + 4, tok(b)], psT[:, n % 4, :].rearrange("p (k t) -> p k t", k=4))\
                    .then_inc(hh_done, 1)

        def act_hi(fc):
            act.wait_ge(af_done, fc + 1)
            if fc >= FT:
                act.wait_ge(d_ps, 8)
            a_.copy(aTh[:, fc % FT, :], af[fc % 2][:]).then_inc(ah_done, 1)

        for o in range(O_STEPS):
            for n in (w2.due(M_STEPS + o - 1, RING) if o else []):
                w2.split_hi(act, n)
            for b in range(HT):
                if o == TURN_AT[b] + 1:
                    turned_h(b)
            if o == O_STEPS - 1:
                for n in w2.due(M_STEPS + o, RING):
                    w2.split_hi(act, n)
            if o >= NT:
                act.wait_ge(h_done, o + 1)
                squared(0, o - NT, squares[:])
            if o == O_STEPS - HT - 1:
                root(0, slice(0, HT), 1)
        root(0, slice(HT, NT), 2)
        for t in range(2):
            step = M_STEPS + O_STEPS + 2 * FT * t
            for f in range(FT):
                fc = FT * t + f
                for n in w2.due(step + f, RING):
                    w2.split_hi(act, n)
                act.wait_ge(f_ps, fc + 1)
                if fc >= 2:
                    act.wait_ge(af_done, fc - 1)
                if f < 2:
                    act.wait_ge(ht_ps, 2 * HT * (t + 1))
                a_.activation(sg[fc % 2][:], psA[:, 2 * (fc % 2), :], ACT.Silu).then_inc(sg_done, 1)
                if f >= 1:
                    act_hi(fc - 1)
                if t == 1 and f < HT:
                    if f == 0:
                        act.wait_ge(d_done, 8)
                    squared(1, f, psT2[:, f % 2, :])
                if t == 1 and f == OUT_AT - 1:
                    root(1, slice(0, HT), 3)
            act_hi(FT * t + FT - 1)
            for a in range(FT):
                for n in w2.due(step + FT + a, RING):
                    w2.split_hi(act, n)
                if t == 0 and a % 2 and a // 2 < HT:
                    turned_h(HT + a // 2)
        for b in range(HT):
            act.wait_ge(d_done, 12 + b + 1)
            if b >= 2:
                act.wait_ge(hq_done, NT + HT + b - 1)
            squared(1, HT + b, psA2[:, b % 2, :])
            root(1, slice(HT + b, HT + b + 1), 4 + b)

    @block.tensor
    def _(pe):
        def three(ps, pairs, start=True, stop=True):
            for n, ((ah, al), (bh, bl)) in enumerate(pairs):
                first, last = start and n == 0, stop and n == len(pairs) - 1
                pe.matmul(ps, ah, bh, start=first, stop=False)
                pe.matmul(ps, ah, bl, start=False, stop=False)
                mm = pe.matmul(ps, al, bh, start=False, stop=last)
            return mm

        def turn4(bank, blocks):
            for n, src in enumerate(blocks):
                mm = pe.transpose(bank[:, P * n:P * (n + 1)], src, ident[:])
            return mm

        pe.wait_ge(consts, 2)
        for n in range(NA):
            i, g = n // 2, n % 2
            pe.wait_ge(xs_done, i + 1)
            if n >= 4:
                pe.wait_ge(xl_done, n - 3)
            turn4(psT[:, n % 4, :], [xs[i % 2][:, P * k:P * (k + 1)] for k in range(4 * g, 4 * g + 4)]).then_inc(xt_ps, 1)

        def z_step(q):
            c, i = zsteps[q]
            width = COLS[c][1]
            if q >= 4:
                pe.wait_ge(z_out, q - 3)
            if q == NT:
                pe.wait_ge(sc_done, len(iunits))
            if q == 0:
                pe.wait_ge(xl_done, NA)
            for a in range(KT // 2):
                n = 4 * (q // NT) + a
                if i == 0:
                    pe.wait_ge(w1.lo_done, n + 1)
                hi, lo = w1.parts(n, 2)
                mm = three(psA[:, q % 4, 0:width],
                           [((xTh[:, 2 * a + k, tok(i)], xTl[:, 2 * a + k, tok(i)]), (hi[:, k, :], lo[:, k, :]))
                            for k in range(2)], a == 0, a == KT // 2 - 1)
                if i == NT - 1 and a < KT // 2 - 1:
                    mm.then_inc(w1.freed, 1)
            mm.then_inc(z_ps, 1)

        def z_turn(q):
            c, i = zsteps[q]
            pe.wait_ge(bl_done, q + 1)
            for g, n in enumerate(GROUPS[c]):
                k = turned[q, g]
                if k > 4:
                    pe.wait_ge(zt_out, k - 4)
                src = [blk[q % 2][:, 4 * g + b, :].bitcast(F32) for b in range(n)]
                if c == CMP and g == 1:
                    src = [kcvc[q % 2][:, P * b:P * (b + 1)] for b in range(2)]
                turn4(psT[:, (NA + k - 1) % 4, :], src).then_inc(zt_ps, 1)

        def stage2(first, stop):
            for q in range(first, stop + 2):
                if q < stop:
                    z_step(q)
                if first <= q - 2 < stop:
                    z_turn(q - 2)

        def scores(ps, q_, k_hi, k_lo, n):
            for c0, c1 in seg(n):
                pe.matmul(ps[:, c0:c1], q_, k_hi[:, c0:c1], start=True, stop=False)
                mm = pe.matmul(ps[:, c0:c1], q_, k_lo[:, c0:c1], start=False, stop=True)
            return mm

        stage2(0, NT)
        pe.wait_ge(zt_out, turned[NT - 1, 1])
        pe.wait_ge(z_out, NT)
        for v, (i, h) in enumerate(iunits):
            if v >= 2:
                pe.wait_ge(sc_done, v - 1)
            scores(psA2[:, v % 2, :], iqT[:, h, tok(i)], ikT[:, 0, :], ikT[:, 1, :], i + 1).then_inc(id_ps, 1)
        stage2(NT, Z_STEPS)
        for g in range(G_STEPS):
            n, half = NCH + g // 2, slice(HALF * (g % 2), HALF * (g % 2 + 1))
            pe.wait_ge(w1.lo_done, n + 1)
            if g < 4:
                pe.wait_ge(z_out, Z_STEPS - 3 + g)
            else:
                pe.wait_ge(g_out, g - 3)
            hi, lo = w1.parts(n, KT)
            three(psA[:, g % 4, :], [((hi[:, k, :], lo[:, k, :]), (xTh[:, k, half], xTl[:, k, half]))
                                     for k in range(KT)]).then_inc(g_ps, 1)

        pe.wait_ge(g_out, G_STEPS)
        pe.wait_ge(zt_out, len(turned))

        def group(key):
            n = g6[key]
            if n >= 2:
                before = groups6[n - 2]
                pe.wait_ge(*((t_act, act_took[before]) if by_act(before) else (t_dve, dve_took[before])))
            return psT[:, n % 2, :]

        def accumulator(key):
            n = o6[key]
            if n >= 2:
                pe.wait_ge(o_out, o_took[opened[n - 2]])
            return psT[:, 2 + n % 2, :]

        for u in range(STEPS6):
            v = u - T_LAG
            a, i, h = at(v)
            if a:
                pe.wait_ge(p_done, v + 1)
                for g, (c0, c1) in enumerate(seg(keys_of(a, i)[1])):
                    turn4(group(("p", v, g)), [p_sb[v % PR][:, c:c + P] for c in range(c0, c1, P)]).then_inc(t_ps, 1)
            a, i, h = at(u)
            if a:
                if u == ND:
                    pe.wait_ge(kT_in, 32)
                if u >= 2:
                    pe.wait_ge(s_done, u - 1)
                k0, n = keys_of(a, i)
                cols = slice(P * k0, P * (k0 + n))
                if a == "dsa":
                    if h == 0:
                        pe.wait_ge(q_in[i % 2], 16 * (i // 2 + 1))
                    mm = scores(psA2[:, u % 2, :], qt[i % 2][:, h, :], kbT[:, 0, cols], kbT[:, 1, cols], n)
                else:
                    if a == "win" and h == 0:
                        pe.wait_ge(q_in[i % 2], 16 * ((NT + i) // 2 + 1))
                    kk = kT[a]
                    mm = scores(psA2[:, u % 2, :], qt[i % 2][:, h, :], kk[:, h // G, 0, cols], kk[:, h // G, 1, cols], n)
                mm.then_inc(s_ps, 1)
            v = u - V_LAG
            a, i, h = at(v)
            if a:
                k0, n = keys_of(a, i)
                for g in range(len(seg(n))):
                    key = ("p", v, g)
                    pe.wait_ge(*((t_act, act_took[key]) if by_act(key) else (t_dve, dve_took[key])))
                bank = accumulator((a, i)) if h == 0 else psT[:, 2 + o6[a, i] % 2, :]
                for k in range(n):
                    if a == "dsa":
                        val = v_b[:, k0 + k, :]
                    else:
                        val = (v_slc if a == "slc" else v_win)[:, k0 + k, HD * (h // G):HD * (h // G + 1)]
                    mm = pe.matmul(bank[:, HD * h:HD * (h + 1)], pT[v % 2][:, k, :], val, start=(k == 0), stop=(k == n - 1))
                mm.then_inc(pv_ps, 1)
            if u == CH_AT:
                pe.wait_ge(cw_in, 16 * 6)
                bank = group(("ch", 0, 0))
                for n, done in ((0, cx_k), (1, cx_v)):
                    pe.wait_ge(done, 8)
                    for hh in range(HH):
                        for j in range(JP):
                            mm = pe.matmul(bank[:, P * (HH * n + hh):P * (HH * n + hh + 1)], w1c[n][:, j, P * hh:P * (hh + 1)],
                                           xc[n][:, j, :, :].rearrange("p g w -> p (g w)"),
                                           start=(j == 0), stop=(j == JP - 1))
                mm.then_inc(t_ps, 1)
            if u == CK_AT:
                pe.wait_ge(t_act, act_took["ch", 0, 0])
                bank = group(("ck", 0, 0))
                for hh in range(HH):
                    pe.matmul(bank[:, 0:P], w2c[0][:, hh, :, :].rearrange("p r d -> p (r d)"), hid_k[:, hh, :],
                              start=(hh == 0), stop=(hh == HH - 1))
                for g in range(KV):
                    for hh in range(HH):
                        mm = pe.matmul(bank[:, P + HD * g:P + HD * (g + 1)], hid_v[:, hh, g, :, :].rearrange("p r w -> p (r w)"),
                                       w2c[1][:, hh, 0, :], start=(hh == 0), stop=(hh == HH - 1))
                mm.then_inc(t_ps, 1)
            i = cmp_tile(u, 0)
            if i is not None:
                pe.wait_ge(q_in[i % 2], 16 * ((NT + i) // 2 + 1))
                if i == 0:
                    pe.wait_ge(t_dve, dve_took["ck", 0, 0])
                bank = group(("cs", i, 0))
                for h in range(H):
                    ps, q_ = bank[:, HD * h:HD * (h + 1)], qt[i % 2][:, h, :]
                    pe.matmul(ps, q_, kcm[:, h // G, 0, :], start=True, stop=False)
                    mm = pe.matmul(ps, q_, kcm[:, h // G, 1, :], start=False, stop=True)
                mm.then_inc(t_ps, 1)
            i = cmp_tile(u, C_TURN)
            if i is not None:
                pe.wait_ge(cp_done, i + 1)
                turn4(group(("cp", i, 0)), [c_p[:, 2 * n:2 * n + 2, :].rearrange("p a w -> p (a w)") for n in range(4)])\
                    .then_inc(t_ps, 1)
            i = cmp_tile(u, C_OUT)
            if i is not None:
                pe.wait_ge(t_act, act_took["cp", i, 0])
                bank = group(("co", i, 0))
                for n in range(4):
                    mm = pe.matmul(bank[:, P * n:P * (n + 1)], c_pT[:, n, :], vbd[:, 2 * n // G, :], start=True, stop=True)
                mm.then_inc(t_ps, 1)
            if y_of(u):
                a, i = y_of(u)
                pe.wait_ge(*((y_done, 2 * i + 2) if a == "slc" else (o_out, o_took[a, i])))
                y = ya[(ysteps["y", a, i] - 1) % 2]
                turn4(group(("y", a, i)), [y[:, P * k:P * (k + 1)] for k in range(4)]).then_inc(t_ps, 1)

        pe.wait_ge(t_dve, len(dve_took))
        pe.wait_ge(s_done, len(units))
        for m in range(M_STEPS):
            j, half = m // 2, slice(HALF * (m % 2), HALF * (m % 2 + 1))
            pe.wait_ge(w2.lo_done, j + 1)
            if m >= 2:
                pe.wait_ge(m_done, m - 1)
            hi, lo = w2.parts(j, KT)
            for b, set_ in enumerate(("nsa", "dsa")):
                mm = three(psA[:, 2 * (m % 2) + b, :],
                           [((hi[:, 4 * b + k, :], lo[:, 4 * b + k, :]), (yTh[set_][:, k, half], yTl[set_][:, k, half]))
                            for k in range(4)])
            mm.then_inc(m_ps, 1)
        def turn_h(i):
            pe.wait_ge(hn_done, i + 1)
            for g in range(2):
                n = 2 * i + g
                if n >= 4:
                    pe.wait_ge(hl_done, n - 3)
                turn4(psT[:, n % 4, :], [hn[i % 2][:, P * k:P * (k + 1)] for k in range(4 * g, 4 * g + 4)])\
                    .then_inc(ht_ps, 1)

        for o in range(O_STEPS):
            n, i = o // NT, o % NT
            if o >= 4:
                pe.wait_ge(h_done, o - 3)
            else:
                pe.wait_ge(m_done, M_STEPS - 1 + o // 2)
            for a in range(KT // 2):
                item = KT + 4 * n + a
                if o == 0:
                    pe.wait_ge(ml_done, 4 * a + 3)
                elif o == HT:
                    pe.wait_ge(ml_done, M_STEPS)
                if i == 0:
                    pe.wait_ge(w2.lo_done, item + 1)
                hi, lo = w2.parts(item, 2)
                mm = three(psA[:, o % 4, :], [((mTh[:, 2 * a + k, tok(i)], mTl[:, 2 * a + k, tok(i)]), (hi[:, k, :], lo[:, k, :]))
                                              for k in range(2)], a == 0, a == KT // 2 - 1)
                if i == NT - 1 and a < KT // 2 - 1:
                    mm.then_inc(w2.freed, 1)
            mm.then_inc(o_ps, 1)
            for b in range(HT):
                if TURN_AT[b] == o:
                    turn_h(b)

        pe.wait_ge(h_done, O_STEPS - 2)
        item = KT + 8
        for t in range(2):
            pe.wait_ge(hl_done, 8 * (t + 1))
            for f in range(FT):
                fc = FT * t + f
                if fc == 1:
                    pe.wait_ge(h_done, O_STEPS)
                if t == 1 and f < 2:
                    pe.wait_ge(d_done, 4)
                if fc >= 2:
                    pe.wait_ge(af_done, fc - 1)
                for b in range(2):
                    pe.wait_ge(w2.lo_done, item + 1)
                    hi, lo = w2.parts(item, KT)
                    mm = three(psA[:, 2 * (fc % 2) + b, :],
                               [((hi[:, k, :], lo[:, k, :]), (hTh[:, k, :], hTl[:, k, :])) for k in range(KT)])
                    item += 1
                mm.then_inc(f_ps, 1)

            def down(n, a, b, item):
                banks, end = psA if n == 0 else psT, a == FT // 2 - 1
                if a == 0:
                    if n == 0:
                        pe.wait_ge(af_done, FT * (t + 1) - 1 + b // 2)
                    elif t == 1:
                        pe.wait_ge(d_done, 8)
                        pe.wait_ge(hd_done, 3)
                    else:
                        pe.wait_ge(hl_done, 2 * NT)
                hi, lo = w2.parts(item, 2)
                mm = three(banks[:, b, :],
                           [((aTh[:, 2 * a + k, tok(b)], aTl[:, 2 * a + k, tok(b)]), (hi[:, k, :], lo[:, k, :]))
                            for k in range(2)], a == 0, end)
                if end:
                    mm.then_inc(d_ps, 1)
                return mm

            for n in range(2):
                together = 3 if (t, n) == (1, 1) else 1
                for a in range(FT // 2 - together + 1):
                    for k in range(together if a == FT // 2 - together else 1):
                        pe.wait_ge(w2.lo_done, item + k + 1)
                    pe.wait_ge(al_done, FT * t + 2 * a + 2)
                    if a == FT // 2 - together:
                        pe.wait_ge(al_done, FT * (t + 1))
                    for b in range(HT):
                        for k in range(together if a == FT // 2 - together else 1):
                            mm = down(n, a + k, b, item + k)
                    if a < FT // 2 - 1 and together == 1 or a < FT // 2 - together:
                        mm.then_inc(w2.freed, 1)
                    item += 1
                    if (t, n) == (0, 0) and a % 2 and a // 2 < HT:
                        turn_h(HT + a // 2)

    @block.vector
    def _(dve):
        v_ = nc.vector
        seq = [0]

        def signal(ins):
            ins.then_inc(dve_seq, 1)
            seq[0] += 1
            return seq[0]

        def then(ins):
            ins.then_inc(dve_seq, 1)
            seq[0] += 1
            dve.wait_ge(dve_seq, seq[0])

        def rstd(st, c):
            then(v_.reciprocal(st[:, 3, c], st[:, 2, c]))
            then(v_.tensor_tensor(st[:, 4, c], st[:, 3, c], st[:, 3, c], ALU.mult))
            then(v_.tensor_tensor(st[:, 4, c], st[:, 4, c], st[:, 1, c], ALU.mult))
            then(v_.tensor_scalar(st[:, 4, c], st[:, 4, c], -0.5, 1.5, ALU.mult, ALU.add))
            then(v_.tensor_tensor(st[:, 3, c], st[:, 3, c], st[:, 4, c], ALU.mult))

        def x_lo(i):
            for n in (2 * i, 2 * i + 1):
                g = n % 2
                dve.wait_ge(xh_done, n + 1)
                v_.tensor_tensor(xTl[:, 4 * g:4 * g + 4, tok(i)], psT[:, n % 4, :].rearrange("p (k t) -> p k t", k=4),
                                 xTh[:, 4 * g:4 * g + 4, tok(i)].bitcast(F32), ALU.subtract).then_inc(xl_done, 1)

        for b in range(2):
            c = slice(HT * b, HT * (b + 1))
            dve.wait_ge(sq_done, HT * (b + 1))
            v_.tensor_scalar(stat[:, 1, c], stat[:, 0, c], 1.0 / D, EPS, ALU.mult, ALU.add).then_inc(var_done, 1)
            dve.wait_ge(var_done, b + 1)
            dve.wait_ge(sd_done, b + 1)
            rstd(stat, c)
            for i in range(HT * b, HT * (b + 1)):
                if i == 0:
                    dve.wait_ge(gain_in, 16)
                if i >= 2:
                    dve.wait_ge(xt_ps, 2 * (i - 1))
                v_.scalar_tensor_tensor(out=xs[i % 2][:], in0=xr[i % XR][:], scalar=stat[:, 3, i:i + 1], in1=gain1[:],
                                        op0=ALU.mult, op1=ALU.mult).then_inc(xs_done, 1)
                if i % HT:
                    x_lo(i - 1)
            x_lo(HT * b + HT - 1)

        def rope(q):
            c, i = zsteps[q]
            z, r = zs[q % 2], ro[q % 2]
            dve.wait_ge(z_out, q + 1)
            if q == 0:
                dve.wait_ge(table_in, 32)
            if q >= 1:
                dve.wait_ge(rope_done, q)
            if q >= 2:
                dve.wait_ge(bh_done, q - 1)
                dve.wait_ge(bl_done, q - 1)
            if c == CMP and cmps[q] > 2:
                dve.wait_ge(zt_ps, turned[q - 2, 1])

            def out_of(col, w):
                return (kcvc[q % 2] if c == CMP and col == 0 else r)[:, col:col + w]

            for col, n in ROPED[c]:
                w = n * HD
                src, tmp = heads(z[:, col:col + w], n), heads(rot[:, col:col + w], n)
                cos = cosT[:, i, :].unsqueeze(1).to_broadcast([P, n, HD])
                v_.tensor_tensor(heads(out_of(col, w), n), src, cos, ALU.mult)
                for lo_, hi_ in ((0, HD // 2), (HD // 2, 0)):
                    sin = sinT[:, i, lo_:lo_ + HD // 2].unsqueeze(1).to_broadcast([P, n, HD // 2])
                    last = v_.tensor_tensor(tmp[:, :, lo_:lo_ + HD // 2], src[:, :, hi_:hi_ + HD // 2], sin, ALU.mult)
            then(last)
            for col, n in ROPED[c]:
                w = n * HD
                last = v_.tensor_tensor(out_of(col, w), out_of(col, w), rot[:, col:col + w], ALU.add)
            last.then_inc(rope_done, 1)

        def block_lo(q):
            c, i = zsteps[q]
            r, t = ro[q % 2], blk[q % 2]
            dve.wait_ge(rope_done, q + 1)
            dve.wait_ge(bh_done, q + 1)
            for col, n, b in QBLK[c]:
                last = v_.tensor_tensor(t[:, b:b + n, HD:P], heads(r[:, col:col + n * HD], n),
                                        t[:, b:b + n, 0:HD].bitcast(F32), ALU.subtract)
            for col, b in KBLK[c]:
                last = v_.tensor_tensor(t[:, b + 1, :].rearrange("p (r d) -> p r d", r=2),
                                        r[:, col:col + HD].unsqueeze(1).to_broadcast([P, 2, HD]),
                                        t[:, b, :].bitcast(F32).rearrange("p (r d) -> p r d", r=2), ALU.subtract)
            last.then_inc(bl_done, 1)

        for q in range(NT + 1):
            if q < NT:
                rope(q)
            if q >= 1:
                block_lo(q - 1)
        dve.wait_ge(consts, N_CONST1)
        for v, (i, h) in enumerate(iunits):
            dve.wait_ge(relu_done, v + 1)
            if v >= 1:
                dve.wait_ge(sc_done, v)
            n = P * (i + 1)
            v_.scalar_tensor_tensor(out=score_of(i), in0=psA2[:, v % 2, 0:n], scalar=iw[:, i, h:h + 1],
                                    in1=causal[:, S - n:S] if h == 0 else score_of(i),
                                    op0=ALU.mult, op1=ALU.add).then_inc(sc_done, 1)

        NTK = len(TK)
        R = slice(0, NTK)

        def counts(threshold):
            done = []
            for n, i in enumerate(TK):
                if n >= 2:
                    dve.wait_ge(dve_seq, done[n - 2])
                done.append(signal(v_.tensor_scalar((tk_gt, tk_eq)[n % 2][:, 0:P * (i + 1)], score_of(i), threshold(n),
                                                    None, ALU.is_ge, ALU.add, accum_out=count[:, n:n + 1])))
            dve.wait_ge(dve_seq, done[-1])

        def bisect_start():
            dve.wait_ge(sc_done, len(iunits))
            counts(lambda n: 0.0)
            v_.memset(bit_cur[:], 0)
            then(v_.tensor_scalar(bit_flip[:, R], count[:, R], float(TOPK), -1.0, ALU.is_lt, ALU.mult))

        def bisect(bit):
            then(v_.tensor_scalar(bit_try[:, R], bit_cur[:, R], 1 << bit, None, ALU.bitwise_or))
            then(v_.tensor_tensor(bit_try[:, R], bit_try[:, R], bit_flip[:, R], ALU.bitwise_xor))
            counts(lambda n: bit_try[:, n:n + 1].bitcast(F32))
            then(v_.tensor_scalar(bit_keep[:, R], count[:, R], float(TOPK), float(1 << bit), ALU.is_ge, ALU.mult))
            then(v_.tensor_tensor(bit_cur[:, R], bit_cur[:, R], bit_keep[:, R], ALU.bitwise_or))

        def selection():
            then(v_.tensor_tensor(bit_try[:, R], bit_cur[:, R], bit_flip[:, R], ALU.bitwise_xor))
            for n, i in enumerate(TK):
                w, t = P * (i + 1), bit_try[:, n:n + 1].bitcast(F32)
                v_.tensor_scalar(tk_gt[:, 0:w], score_of(i), t, None, ALU.is_gt, ALU.add, accum_out=count[:, n:n + 1])
                then(v_.tensor_scalar(tk_eq[:, 0:w], score_of(i), t, None, ALU.is_equal))
                v_.tensor_scalar(need[:, n:n + 1], count[:, n:n + 1], -1.0, float(TOPK), ALU.mult, ALU.add)
                then(v_.tensor_tensor_scan(tk_cum[:, 0:w], tk_eq[:, 0:w], tk_eq[:, 0:w], 0.0, ALU.add, ALU.max))
                then(v_.scalar_tensor_tensor(out=tk_eq[:, 0:w], in0=tk_cum[:, 0:w], scalar=need[:, n:n + 1],
                                             in1=tk_eq[:, 0:w], op0=ALU.is_le, op1=ALU.mult))
                then(v_.tensor_tensor(tk_gt[:, 0:w], tk_gt[:, 0:w], tk_eq[:, 0:w], ALU.add))
                last = v_.tensor_scalar(score_of(i), tk_gt[:, 0:w], 1.0, -NEG, ALU.subtract, ALU.mult)
                last.then_inc(tk_done, 1)
                dve.wait_ge(tk_done, n + 1)

        bisect_start()
        bit = 30
        for q in range(NT, Z_STEPS + 1):
            if q < Z_STEPS:
                rope(q)
            if q > NT:
                block_lo(q - 1)
            if q % 2 == 0 and bit >= 0:
                bisect(bit)
                bit -= 1
        while bit >= 0:
            bisect(bit)
            bit -= 1
        selection()

        def cmp_bias(i):
            dve.wait_ge(t_ps, g6["cs", i, 0] + 1)
            if i == 0:
                dve.wait_ge(consts, N_CONST6)
            v_.tensor_tensor(c_s[:], heads(psT[:, g6["cs", i, 0] % 2, :], H),
                             cmpb[:, i, :].unsqueeze(1).to_broadcast([P, H, 64]), ALU.add).then_inc(t_dve, 1)

        def cmp_max(i):
            dve.wait_ge(t_dve, dve_took["cs", i, 0])
            v_.tensor_reduce(c_st[:, 0, :], c_s[:], X, ALU.max).then_inc(cm_done, 1)

        def cmp_sum(i):
            dve.wait_ge(ce_done, i + 1)
            return signal(v_.tensor_reduce(c_st[:, 1, :], c_p[:], X, ALU.add))

        def cmp_recip(i):
            dve.wait_ge(dve_seq, c_summed[i])
            if i == 0:
                then(v_.reciprocal(c_st[:, 2, :], c_st[:, 1, :]))
                v_.tensor_scalar(c_st[:, 2, :], c_st[:, 2, :], seen[:, 0:1], None, ALU.mult).then_inc(cr_done, 1)
            else:
                dve.wait_ge(cp_done, i)
                v_.reciprocal(c_st[:, 2, :], c_st[:, 1, :]).then_inc(cr_done, 1)

        def block_ranks(i):
            dve.wait_ge(bs_done, i - TOPN // 2 + 1)
            for a in range(KV):
                other = bs[:, a, :].unsqueeze(1).to_broadcast([P, NSLC, NSLC])
                own = bs[:, a, :].unsqueeze(2).to_broadcast([P, NSLC, NSLC])
                v_.tensor_tensor(cmp_a[:, a], other, own, ALU.is_gt)
                last = v_.tensor_tensor(cmp_b[:, a], other, own, ALU.is_equal)
            then(last)
            for a in range(KV):
                last = v_.tensor_tensor(cmp_b[:, a], cmp_b[:, a], lower[:], ALU.mult)
            then(last)
            then(v_.tensor_tensor(cmp_a[:], cmp_a[:], cmp_b[:], ALU.add))
            if i > TOPN // 2:
                dve.wait_ge(sb_done, i - TOPN // 2)
            then(v_.tensor_reduce(rk[:], cmp_a[:], X, ALU.add))
            v_.tensor_scalar(rk[:], rk[:], TOPN - 0.5, NEG, ALU.is_gt, ALU.mult).then_inc(rank_done, 1)

        def unit_scores(u):
            a, i, h = at(u)
            w = P * keys_of(a, i)[1]
            if a == "win":
                bias = winb[:, WIN + P - w:WIN + P]
            elif a == "slc" and 2 * (i + 1) > TOPN:
                bias = slcb[:, h // G, 0:w]
                dve.wait_ge(sb_done, i - TOPN // 2 + 1)
            elif a == "dsa" and i in sc_at:
                bias = score_of(i)
            else:
                bias = causal[:, S - w:S]
            dve.wait_ge(s_ps, u + 1)
            if u >= 2:
                dve.wait_ge(p_done, u - 1)
            v_.tensor_tensor_reduce(out=s_sb[u % 2][:, 0:w], in0=psA2[:, u % 2, 0:w], in1=bias, scale=-(HD ** -0.5),
                                    scalar=3e38, op0=ALU.add, op1=ALU.min,
                                    accum_out=nmax[:, BR[a], i, h:h + 1]).then_inc(s_done, 1)

        def row_recip(a, i):
            dve.wait_ge(p_done, units.index((a, i, H - 1)) + 1)
            return signal(v_.reciprocal(psum_r[:, BR[a], i, :], psum_p[:, BR[a], i, :]))

        def row_gate(a, i):
            branch, r = 1 if a == "slc" else 2, psum_r[:, BR[a], i, :]
            dve.wait_ge(dve_seq, rowed[a, i])
            return signal(v_.tensor_tensor(r, r, nsa_gate[:, i, H * branch:H * (branch + 1)], ALU.mult))

        def scaled(a, i):
            ps = heads(psT[:, 2 + o6[a, i] % 2, :], H)
            r = psum_r[:, BR[a], i, :].unsqueeze(2).to_broadcast([P, H, HD])
            dve.wait_ge(dve_seq, rowed[a, i])
            dve.wait_ge(pv_ps, units.index((a, i, H - 1)) + 1)
            if a == "dsa":
                n = ysteps["y", a, i]
                if n > 2:
                    dve.wait_ge(t_ps, g6[groups_y[n - 3]] + 1)
                target = ya[(n - 1) % 2]
            else:
                if o_took[a, i] > NT + 1:
                    dve.wait_ge(y_done, o_took[a, i] - NT - 1)
                target = yt
            v_.tensor_tensor(heads(target[:], H), ps, r, ALU.mult).then_inc(o_out, 1)

        def cmp_out(i):
            n = ysteps["y", "slc", i]
            dve.wait_ge(t_ps, g6["co", i, 0] + 1)
            if n > 2:
                dve.wait_ge(t_ps, g6[groups_y[n - 3]] + 1)
            v_.tensor_tensor(heads(ya[(n - 1) % 2][:], H), heads(psT[:, g6["co", i, 0] % 2, :], H),
                             nsa_gate[:, i, 0:H].unsqueeze(2).to_broadcast([P, H, HD]), ALU.mult).then_inc(t_dve, 1)

        rowed, c_summed = {}, {}
        for u in range(STEPS6):
            if u - 1 == CK_AT:
                then(v_.memset(vbd[:], 0.0))
                dve.wait_ge(ck_hi, 1)
                bank = psT[:, g6["ck", 0, 0] % 2, :]
                v_.tensor_tensor(kcm[:, :, 1, :], bank[:, 0:P].rearrange("p (g w) -> p g w", g=KV),
                                 kcm[:, :, 0, :].bitcast(F32), ALU.subtract)
                for g in range(KV):
                    for r in range(2):
                        rows = slice(HD * r, HD * (r + 1))
                        last = v_.tensor_copy(vbd[rows, g, HD * r:HD * (r + 1)], bank[rows, P + HD * g:P + HD * (g + 1)])
                last.then_inc(t_dve, 1)
            if cmp_tile(u, C_BIAS) is not None:
                cmp_bias(cmp_tile(u, C_BIAS))
            if cmp_tile(u - 1, C_OUT) is not None:
                cmp_out(cmp_tile(u - 1, C_OUT))
            if y_of(u - 1):
                a, i = y_of(u - 1)
                key, set_ = ("y", a, i), "dsa" if a == "dsa" else "nsa"
                dve.wait_ge(yh_done, ysteps[key])
                v_.tensor_tensor(yTl[set_][:, :, tok(i)], psT[:, g6[key] % 2, :].rearrange("p (k t) -> p k t", k=4),
                                 yTh[set_][:, :, tok(i)].bitcast(F32), ALU.subtract).then_inc(t_dve, 1)
            if at(u - T_LAG)[0]:
                evac_p(dve, v_.tensor_copy, u - T_LAG, False)
            if at(u)[0]:
                unit_scores(u)
            if cmp_tile(u, C_MAX) is not None:
                cmp_max(cmp_tile(u, C_MAX))
            if cmp_tile(u, C_SUM) is not None:
                c_summed[cmp_tile(u, C_SUM)] = cmp_sum(cmp_tile(u, C_SUM))
            if cmp_tile(u, C_RECIP) is not None:
                cmp_recip(cmp_tile(u, C_RECIP))
            i = cmp_tile(u, C_RANK)
            if i is not None and i >= TOPN // 2:
                block_ranks(i)
            a, i, h = at(u - T_LAG)
            if a and h == H - 1:
                rowed[a, i] = row_recip(a, i)
            a, i, h = at(u - V_LAG)
            if a in ("win", "slc") and h == H - 1:
                rowed[a, i] = row_gate(a, i)
            a, i, h = at(u - F_LAG)
            if a and h == H - 1:
                scaled(a, i)

        def merged_lo(m):
            j, half = m // 2, slice(HALF * (m % 2), HALF * (m % 2 + 1))
            dve.wait_ge(mh_done, m + 1)
            v_.tensor_tensor(mTl[:, j, half], mf[m % 2][:], mTh[:, j, half].bitcast(F32), ALU.subtract).then_inc(ml_done, 1)

        for m in range(M_STEPS):
            dve.wait_ge(m_ps, m + 1)
            dve.wait_ge(gl_in[m % 2], 32 * (m // 2 + 1))
            if m >= 1:
                dve.wait_ge(m_done, m)
            v_.tensor_tensor(ma[:], psA[:, 2 * (m % 2), :], gl[m % 2][:, 0, :], ALU.mult)
            then(v_.tensor_tensor(mb[:], psA[:, 2 * (m % 2) + 1, :], gl[m % 2][:, 1, :], ALU.mult))
            if m >= 2:
                dve.wait_ge(mh_done, m - 1)
                dve.wait_ge(ml_done, m - 1)
            v_.tensor_tensor(mf[m % 2][:], ma[:], mb[:], ALU.add).then_inc(m_done, 1)
            if m >= 1:
                merged_lo(m - 1)
        merged_lo(M_STEPS - 1)
        def rooted(r, c, n, squares_done):
            dve.wait_ge(hq_done, squares_done)
            v_.tensor_scalar(hstat[:, r, 1, c], hstat[:, r, 0, c], 1.0 / D, EPS, ALU.mult, ALU.add).then_inc(hv_done, 1)
            dve.wait_ge(hv_done, n)
            dve.wait_ge(hd_done, n)
            rstd(hstat[:, r], c)

        def normed(i):
            if i >= 2:
                dve.wait_ge(ht_ps, 2 * (i - 1))
            v_.scalar_tensor_tensor(out=hn[i % 2][:], in0=hrow[:, i, :], scalar=hstat[:, 0, 3, i:i + 1], in1=gain2[:],
                                    op0=ALU.mult, op1=ALU.mult).then_inc(hn_done, 1)

        def h_lo(i):
            for g in range(2):
                n = 2 * i + g
                dve.wait_ge(hh_done, n + 1)
                v_.tensor_tensor(hTl[:, 4 * g:4 * g + 4, tok(i % HT)], psT[:, n % 4, :].rearrange("p (k t) -> p k t", k=4),
                                 hTh[:, 4 * g:4 * g + 4, tok(i % HT)].bitcast(F32), ALU.subtract).then_inc(hl_done, 1)

        def act_lo(fc):
            dve.wait_ge(ah_done, fc + 1)
            v_.tensor_tensor(aTl[:, fc % FT, :], af[fc % 2][:], aTh[:, fc % FT, :].bitcast(F32), ALU.subtract)\
                .then_inc(al_done, 1)

        def scaled_out(i):
            v_.scalar_tensor_tensor(out=hrow[:, i, :], in0=hrow[:, i, :], scalar=hstat[:, 1, 3, i:i + 1],
                                    in1=gain2[:], op0=ALU.mult, op1=ALU.mult).then_inc(out_ready, 1)

        def down_sum(t, n, b):
            dve.wait_ge(d_ps, 8 * t + 4 * n + b + 1)
            piece = hrow[:, HT * t + b, 512 * n:512 * (n + 1)]
            v_.tensor_tensor(piece, piece, (psA if n == 0 else psT)[:, b, :], ALU.add).then_inc(d_done, 1)

        for o in range(O_STEPS):
            n, i = o // NT, o % NT
            for b in range(HT):
                if o == TURN_AT[b] + 1:
                    h_lo(b)
                    if b + 2 < HT:
                        normed(b + 2)
            dve.wait_ge(o_ps, o + 1)
            dve.wait_ge(xl_in[o % 2], 16 * (o // 2 + 1))
            v_.tensor_tensor(hrow[:, i, 512 * n:512 * (n + 1)], psA[:, o % 4, :], xl[o % 2], ALU.add).then_inc(h_done, 1)
            if o == O_STEPS - HT - 1:
                rooted(0, slice(0, HT), 1, HT)
                dve.wait_ge(gain_in, 32)
                normed(0)
                normed(1)
        rooted(0, slice(HT, NT), 2, NT)

        for t in range(2):
            for f in range(FT):
                fc = FT * t + f
                dve.wait_ge(sg_done, fc + 1)
                if f < 2:
                    dve.wait_ge(ht_ps, 2 * HT * (t + 1))
                if fc >= 2:
                    dve.wait_ge(ah_done, fc - 1)
                    dve.wait_ge(al_done, fc - 1)
                v_.tensor_tensor(af[fc % 2][:], sg[fc % 2][:], psA[:, 2 * (fc % 2) + 1, :], ALU.mult).then_inc(af_done, 1)
                if f >= 1:
                    act_lo(fc - 1)
                if t == 1 and f == OUT_AT - 1:
                    rooted(1, slice(0, HT), 3, NT + HT)
                    dve.wait_ge(gain_in, 48)
                if t == 1 and OUT_AT <= f < OUT_AT + HT:
                    scaled_out(f - OUT_AT)
            act_lo(FT * t + FT - 1)
            if t == 0:
                dve.wait_ge(al_done, FT)
                normed(HT)
                normed(HT + 1)
                for b in range(HT):
                    h_lo(HT + b)
                    if b + 2 < HT:
                        normed(HT + b + 2)
            for n in range(2):
                for b in range(HT):
                    down_sum(t, n, b)
                    if (t, n) == (1, 1):
                        rooted(1, slice(HT + b, HT + b + 1), 4 + b, NT + HT + b + 1)
                        scaled_out(HT + b)

    ctx.close()


INS = ["x", "norm_mix", "w_in", "cmp_pos_k", "cmp_w1_k", "cmp_w2_k", "cmp_pos_v", "cmp_w1_v", "cmp_w2_v",
       "w_branch_nsa", "w_branch_dsa", "w_out", "norm_ffn", "w_gate", "w_up", "w_down", "norm_final"]


def rope_tables(seq):
    half = HD // 2
    freq = (10000.0 ** (-np.arange(half, dtype=np.float64) / half)).astype(np.float32)
    angle = np.arange(seq, dtype=np.float32)[:, None] * freq[None, :]
    cos, sin = np.cos(angle), np.sin(angle)
    return np.concatenate([cos, cos], 1), np.concatenate([-sin, sin], 1)


def kernel(**inputs):
    import concourse.bacc as bacc
    from concourse.bass_utils import run_bass_kernel_spmd

    nc = bacc.Bacc("TRN2", target_bir_lowering=False, num_devices=1)
    arrays = {name: np.ascontiguousarray(inputs[name]) for name in INS}
    seq, d = arrays["x"].shape[1:]
    arrays["rope_cos"], arrays["rope_sin"] = rope_tables(seq)
    feeds = {f"in_{name}_dram": a for name, a in arrays.items()}
    A = {name: nc.dram_tensor(f"in_{name}_dram", a.shape, F32, kind="ExternalInput").ap() for name, a in arrays.items()}
    out = nc.dram_tensor("out_dram", (1, seq, d), F32, kind="ExternalOutput").ap()
    nt = seq // P
    scratch = {name: nc.dram_tensor(f"scratch_{name}", shape, F32, kind="Internal").ap() for name, shape in {
        "q_nsa": (nt, P, 8 * P), "q_dsa": (nt, P, 8 * P), "k_slc": (P, 4, seq), "k_win": (P, 4, seq),
        "gates": (2 * d // P, P, seq)}.items()}
    hybrid_block(nc, A, out, scratch)
    r = run_bass_kernel_spmd(nc, [feeds], core_ids=[0])
    return np.asarray(r.results[0]["out_dram"])
```
